# Optimizing a Trainium2 kernel written in Bass

```python
import functools
import jax, jax.numpy as jnp
from jax import lax
import numpy as np

D_MODEL = 1024
BATCH = 1
SEQ = 2048
DEPTH = 1
DEC_BATCH = 8
DEC_SEQ = 8
PAST_LEN = 4096
PAGE_SIZE = 128

HEAD_DIM = 64
H_A = 4
H_B = 6
H_C = 6
D_A = H_A * HEAD_DIM
D_B = H_B * HEAD_DIM
D_C = H_C * HEAD_DIM
D_MIX = D_A + D_B + D_C
D_FF = 4 * D_MODEL
DILATIONS = ((128, 1), (512, 4), (2048, 16))
MAX_WINDOW = 2048
BLK = 128
MLSTM_CHUNK = 128
RMS_EPS = 1e-6
SB_BIAS_INIT = -8.0
PROJ_SIZES = (D_A, D_A, D_A, D_A, H_A, H_A, D_B, D_B, D_B, D_C, D_C, D_C)
PROJ_COLS = sum(PROJ_SIZES)

kernel_name = 'hymba_mlstm_dilated_stickbreaking_step'

def rmsnorm(x, g):
    x32 = x.astype(jnp.float32)
    r = lax.rsqrt(jnp.mean(x32 * x32, axis=-1, keepdims=True) + RMS_EPS)
    return (x32 * r * g.astype(jnp.float32)).astype(x.dtype)

def project(h, w_in, b_igate, b_fgate):
    B, T, _ = h.shape
    p = jnp.einsum('btd,dc->btc', h, w_in).astype(jnp.float32)
    splits = np.cumsum(PROJ_SIZES)[:-1].tolist()
    qa, ka, va, oa, ia, fa, qb, kb, vb, qc, kc, vc = jnp.split(p, splits, axis=-1)
    heads = lambda a, H: a.reshape(B, T, H, HEAD_DIM)
    ig = ia + b_igate.astype(jnp.float32)
    lf = jax.nn.log_sigmoid(fa + b_fgate.astype(jnp.float32))
    return (heads(qa, H_A), heads(ka, H_A), heads(va, H_A), oa, ig, lf,
            heads(qb, H_B), heads(kb, H_B), heads(vb, H_B),
            heads(qc, H_C), heads(kc, H_C), heads(vc, H_C))

def mlstm_chunk(carry, xs):
    C, n, m = carry
    q, k, v, ig, lf = xs
    L = q.shape[2]
    b = jnp.cumsum(lf, axis=-1)
    causal = jnp.tril(jnp.ones((L, L), dtype=bool))
    logw = jnp.where(causal, b[..., :, None] - b[..., None, :] + ig[..., None, :], -jnp.inf)
    m_inter = b + m[..., None]
    m_t = jnp.maximum(m_inter, jnp.max(logw, axis=-1))
    w_inter = jnp.exp(m_inter - m_t)
    s = jnp.einsum('bhtd,bhsd->bhts', q, k) * jnp.exp(logw - m_t[..., None])
    num = w_inter[..., None] * jnp.einsum('bhed,bhtd->bhte', C, q) + jnp.einsum('bhts,bhse->bhte', s, v)
    den = w_inter * jnp.einsum('bhd,bhtd->bht', n, q) + jnp.sum(s, axis=-1)
    h = num / jnp.maximum(jnp.abs(den), jnp.exp(-m_t))[..., None]
    m_new = m_t[..., -1]
    decay = jnp.exp(b[..., -1] + m - m_new)
    w_end = jnp.exp(b[..., -1:] - b + ig - m_new[..., None])
    C_new = decay[..., None, None] * C + jnp.einsum('bhs,bhse,bhsd->bhed', w_end, v, k)
    n_new = decay[..., None] * n + jnp.einsum('bhs,bhsd->bhd', w_end, k)
    return (C_new, n_new, m_new), h

def mlstm(q, k, v, ig, lf, C0, n0, m0, chunk):
    B, T, H, D = q.shape
    nc = T // chunk
    k = k * D ** -0.5

    def chunks(a):
        a = a.reshape((B, nc, chunk, H) + a.shape[3:])
        return jnp.moveaxis(a, (1, 3), (0, 2))

    (C, n, m), h = lax.scan(mlstm_chunk, (C0, n0, m0),
                            (chunks(q), chunks(k), chunks(v), chunks(ig), chunks(lf)))
    h = jnp.moveaxis(h, (0, 2), (1, 3)).reshape(B, T, H, D)
    return h, C, n, m

def combine_branches(outs, lses):
    w = jax.nn.softmax(jnp.stack(lses), axis=0)
    return jnp.einsum('gbth,gbthe->bthe', w, jnp.stack(outs))

def dilated_prompt(q, k, v):
    B, S, H, D = q.shape
    scale = D ** -0.5
    outs, lses = [], []
    for window, dil in DILATIONS:
        reach = window // dil
        span = dil * BLK
        s_pad = -(-S // span) * span
        nb = s_pad // span

        def blocks(a):
            a = jnp.pad(a, ((0, 0), (0, s_pad - S), (0, 0), (0, 0)))
            return a.reshape(B, nb, BLK, dil, H, D)

        qs, ks, vs = blocks(q), blocks(k), blocks(v)

        def with_prev(a):
            prev = jnp.concatenate([jnp.zeros_like(a[:, :1]), a[:, :-1]], axis=1)
            return jnp.concatenate([prev, a], axis=2)

        kk, vv = with_prev(ks), with_prev(vs)
        qi = jnp.arange(BLK)[:, None] + BLK
        kj = jnp.arange(2 * BLK)[None, :]
        band = (qi - kj >= 0) & (qi - kj <= reach)
        valid = band[None] & ((jnp.arange(nb)[:, None, None] > 0) | (kj >= BLK)[None])
        s = jnp.einsum('bnirhe,bnjrhe->bnrhij', qs, kk) * scale
        s = jnp.where(valid[None, :, None, None], s, -jnp.inf)
        mx = jnp.max(s, axis=-1, keepdims=True)
        p = jnp.exp(s - mx)
        den = jnp.sum(p, axis=-1)
        o = jnp.einsum('bnrhij,bnjrhe->bnirhe', p, vv) / jnp.moveaxis(den, -1, 2)[..., None]
        lse = jnp.moveaxis(mx[..., 0] + jnp.log(den), -1, 2)
        outs.append(o.reshape(B, s_pad, H, D)[:, :S])
        lses.append(lse.reshape(B, s_pad, H)[:, :S])
    return combine_branches(outs, lses)

def dilated_sample(q, k, v, buf_k, buf_v):
    B, T, H, D = q.shape
    scale = D ** -0.5
    wb = buf_k.shape[1]
    k_all = jnp.concatenate([buf_k.astype(jnp.float32), k], axis=1)
    v_all = jnp.concatenate([buf_v.astype(jnp.float32), v], axis=1)
    outs, lses = [], []
    for window, dil in DILATIONS:
        j = jnp.arange(window // dil + 1)
        idx = wb + jnp.arange(T)[:, None] - dil * j[None, :]
        valid = idx >= 0
        idx = jnp.maximum(idx, 0)
        kg = k_all[:, idx]
        vg = v_all[:, idx]
        s = jnp.einsum('bthe,btjhe->bthj', q, kg) * scale
        s = jnp.where(valid[None, :, None, :], s, -jnp.inf)
        mx = jnp.max(s, axis=-1, keepdims=True)
        p = jnp.exp(s - mx)
        den = jnp.sum(p, axis=-1)
        outs.append(jnp.einsum('bthj,btjhe->bthe', p, vg) / den[..., None])
        lses.append(mx[..., 0] + jnp.log(den))
    return combine_branches(outs, lses), k_all[:, T:], v_all[:, T:]

def stick_breaking(q, k, v, b_sb, q_pos, k_pos):
    scale = q.shape[-1] ** -0.5
    z = jnp.einsum('bthe,bshe->bhts', q, k) * scale + b_sb.astype(jnp.float32)[None, :, None, None]
    mask = k_pos[None, :] < q_pos[:, None]
    log_stay = jnp.where(mask, jax.nn.log_sigmoid(-z), 0.0)
    later = lax.cumsum(log_stay, axis=3, reverse=True) - log_stay
    a = jnp.where(mask, jnp.exp(jax.nn.log_sigmoid(z) + later), 0.0)
    return jnp.einsum('bhts,bshe->bthe', a, v)

def sb_prompt(q, k, v, b_sb):
    B, S, H, D = q.shape
    nb = S // BLK
    qb = jnp.moveaxis(q.reshape(B, nb, BLK, H, D), 1, 0)
    pos = jnp.arange(S).reshape(nb, BLK)
    kpos = jnp.arange(S)
    out = lax.map(lambda a: stick_breaking(a[0], k, v, b_sb, a[1], kpos), (qb, pos))
    return jnp.moveaxis(out, 0, 1).reshape(B, S, H, D)

def prompt_mixers(qa, ka, va, ig, lf, qb, kb, vb, qc, kc, vc, b_sb):
    B, S = qa.shape[:2]
    C0 = jnp.zeros((B, H_A, HEAD_DIM, HEAD_DIM), jnp.float32)
    n0 = jnp.zeros((B, H_A, HEAD_DIM), jnp.float32)
    m0 = jnp.zeros((B, H_A), jnp.float32)
    h_a, C, n, m = mlstm(qa, ka, va, ig, lf, C0, n0, m0, min(MLSTM_CHUNK, S))
    y_b = dilated_prompt(qb, kb, vb)
    y_c = sb_prompt(qc, kc, vc, b_sb)
    wb = min(MAX_WINDOW, S)
    return h_a, y_b, y_c, (C, n, m, kb[:, S - wb:], vb[:, S - wb:], kc, vc)

def sample_mixers(C0, n0, m0, buf_k, buf_v, pool_k, pool_v, page_table,
                  qa, ka, va, ig, lf, qb, kb, vb, qc, kc, vc, b_sb):
    Bd, T = qa.shape[:2]
    h_a, C, n, m = mlstm(qa, ka, va, ig, lf, C0.astype(jnp.float32), n0.astype(jnp.float32),
                         m0.astype(jnp.float32), T)
    y_b, new_bk, new_bv = dilated_sample(qb, kb, vb, buf_k, buf_v)
    P = page_table.shape[1] * PAGE_SIZE
    past_k = pool_k[page_table].reshape(Bd, P, H_C, HEAD_DIM).astype(jnp.float32)
    past_v = pool_v[page_table].reshape(Bd, P, H_C, HEAD_DIM).astype(jnp.float32)
    k_all = jnp.concatenate([past_k, kc], axis=1)
    v_all = jnp.concatenate([past_v, vc], axis=1)
    y_c = stick_breaking(qc, k_all, v_all, b_sb, P + jnp.arange(T), jnp.arange(P + T))
    return h_a, y_b, y_c, (C, n, m, new_bk, new_bv, kc, vc)

def merge(h_a, o_gate, y_b, y_c, g_mlstm, w_out, dtype):
    B, T = h_a.shape[:2]
    ha = h_a * lax.rsqrt(jnp.mean(h_a * h_a, axis=-1, keepdims=True) + RMS_EPS)
    ha = ha * g_mlstm.astype(jnp.float32).reshape(H_A, HEAD_DIM)
    ya = ha.reshape(B, T, D_A) * jax.nn.sigmoid(o_gate)
    y = jnp.concatenate([ya, y_b.reshape(B, T, D_B), y_c.reshape(B, T, D_C)], axis=-1).astype(dtype)
    return jnp.einsum('btc,cd->btd', y, w_out)

def sandwich_layer(x, mixer, w_in, b_igate, b_fgate, b_sb, g_mlstm, w_out,
                   g_pre_mix, g_post_mix, g_pre_mlp, g_post_mlp, w_up, w_down):
    h = rmsnorm(x, g_pre_mix)
    qa, ka, va, oa, ig, lf, qb, kb, vb, qc, kc, vc = project(h, w_in, b_igate, b_fgate)
    h_a, y_b, y_c, state = mixer(qa, ka, va, ig, lf, qb, kb, vb, qc, kc, vc, b_sb)
    x = x + rmsnorm(merge(h_a, oa, y_b, y_c, g_mlstm, w_out, x.dtype), g_post_mix)
    u = jax.nn.relu(jnp.einsum('btd,df->btf', rmsnorm(x, g_pre_mlp), w_up))
    x = x + rmsnorm(jnp.einsum('btf,fd->btd', jnp.square(u), w_down), g_post_mlp)
    return x, state

def setup_inputs(seed: int = 0) -> dict:
    key = jax.random.key(seed)
    ks = jax.random.split(key, 24)
    nrm = jax.random.normal
    n_pages = PAST_LEN // PAGE_SIZE
    n_phys = (DEC_BATCH * n_pages * 5) // 4
    wb = min(MAX_WINDOW, PAST_LEN)
    page_table = jax.random.permutation(ks[9], n_phys)[:DEC_BATCH * n_pages]
    page_table = page_table.reshape(DEC_BATCH, n_pages).astype(jnp.int32)
    return {
        'x_prompt': nrm(ks[0], (BATCH, SEQ, D_MODEL), jnp.float32),
        'x_sample': nrm(ks[1], (DEC_BATCH, DEC_SEQ, D_MODEL), jnp.float32),
        'state_mlstm_c': 0.1 * nrm(ks[2], (DEPTH, DEC_BATCH, H_A, HEAD_DIM, HEAD_DIM), jnp.float32),
        'state_mlstm_n': 0.5 * nrm(ks[3], (DEPTH, DEC_BATCH, H_A, HEAD_DIM), jnp.float32),
        'state_mlstm_m': 0.5 * nrm(ks[4], (DEPTH, DEC_BATCH, H_A), jnp.float32),
        'cache_win_k': nrm(ks[5], (DEPTH, DEC_BATCH, wb, H_B, HEAD_DIM), jnp.float32),
        'cache_win_v': nrm(ks[6], (DEPTH, DEC_BATCH, wb, H_B, HEAD_DIM), jnp.float32),
        'cache_sb_k': nrm(ks[7], (DEPTH, n_phys, PAGE_SIZE, H_C, HEAD_DIM), jnp.float32),
        'cache_sb_v': nrm(ks[8], (DEPTH, n_phys, PAGE_SIZE, H_C, HEAD_DIM), jnp.float32),
        'page_table': page_table,
        'w_in': nrm(ks[10], (DEPTH, D_MODEL, PROJ_COLS), jnp.float32) * D_MODEL ** -0.5,
        'b_igate': 0.1 * nrm(ks[11], (DEPTH, H_A), jnp.float32),
        'b_fgate': 3.0 + 0.1 * nrm(ks[12], (DEPTH, H_A), jnp.float32),
        'b_sb': SB_BIAS_INIT + 0.1 * nrm(ks[21], (DEPTH, H_C), jnp.float32),
        'g_mlstm': 1.0 + 0.05 * nrm(ks[13], (DEPTH, D_A), jnp.float32),
        'w_out': nrm(ks[14], (DEPTH, D_MIX, D_MODEL), jnp.float32) * D_MIX ** -0.5,
        'g_pre_mix': 1.0 + 0.05 * nrm(ks[15], (DEPTH, D_MODEL), jnp.float32),
        'g_post_mix': 1.0 + 0.05 * nrm(ks[16], (DEPTH, D_MODEL), jnp.float32),
        'g_pre_mlp': 1.0 + 0.05 * nrm(ks[17], (DEPTH, D_MODEL), jnp.float32),
        'g_post_mlp': 1.0 + 0.05 * nrm(ks[18], (DEPTH, D_MODEL), jnp.float32),
        'w_up': nrm(ks[19], (DEPTH, D_MODEL, D_FF), jnp.float32) * D_MODEL ** -0.5,
        'w_down': nrm(ks[20], (DEPTH, D_FF, D_MODEL), jnp.float32) * D_FF ** -0.5,
    }

def reference(x_prompt, x_sample, state_mlstm_c, state_mlstm_n, state_mlstm_m,
              cache_win_k, cache_win_v, cache_sb_k, cache_sb_v, page_table,
              w_in, b_igate, b_fgate, b_sb, g_mlstm, w_out,
              g_pre_mix, g_post_mix, g_pre_mlp, g_post_mlp, w_up, w_down):
    xp, xs = x_prompt, x_sample
    new_p, new_s = [], []
    for l in range(DEPTH):
        lw = (w_in[l], b_igate[l], b_fgate[l], b_sb[l], g_mlstm[l], w_out[l],
              g_pre_mix[l], g_post_mix[l], g_pre_mlp[l], g_post_mlp[l], w_up[l], w_down[l])
        xp, sp = sandwich_layer(xp, prompt_mixers, *lw)
        smix = functools.partial(sample_mixers, state_mlstm_c[l], state_mlstm_n[l], state_mlstm_m[l],
                                 cache_win_k[l], cache_win_v[l], cache_sb_k[l], cache_sb_v[l], page_table)
        xs, ss = sandwich_layer(xs, smix, *lw)
        new_p.append(sp)
        new_s.append(ss)
    st = lambda states, i: jnp.stack([s[i] for s in states])
    return (xp, xs,
            st(new_p, 0), st(new_p, 1), st(new_p, 2), st(new_p, 3), st(new_p, 4), st(new_p, 5), st(new_p, 6),
            st(new_s, 0), st(new_s, 1), st(new_s, 2), st(new_s, 3), st(new_s, 4), st(new_s, 5), st(new_s, 6))


_drawn_inputs = setup_inputs


def setup_inputs(seed=0):
    import zlib

    import numpy as np

    out = dict(_drawn_inputs(seed))
    spreads = {}
    factors = {'b_sb': 8.0}
    for name, (base, spread) in spreads.items():
        noise = np.random.default_rng([zlib.crc32(name.encode()), seed]).standard_normal(out[name].shape)
        drawn = base * np.exp(spread * noise) if base else spread * noise
        out[name] = __import__('jax').numpy.asarray(drawn.astype(out[name].dtype))
    for name, factor in factors.items():
        out[name] = (out[name] * factor).astype(out[name].dtype)
    return out
```

```python
from contextlib import ExitStack

import concourse.bass as bass
from concourse import mybir

F32 = mybir.dt.float32
F32R = mybir.dt.float32r
I32 = mybir.dt.int32
ALU = mybir.AluOpType
ACT = mybir.ActivationFunctionType
AX = mybir.AxisListType

P = 128
D = 1024
KD = D // P
HD = 64
HA, HB, HC = 4, 6, 6
NA, NB, NC = HA * HD, HB * HD, HC * HD
SEQ = 2048
NT = SEQ // P
DB, DT = 8, 8
NS = DB * DT
TP = SEQ + P
FF = 4 * D
KF = FF // P
WIN = 2048
PAGES, PAGE = 32, 128
EPS = 1e-6
NEG = -1e30
SCALE = HD ** -0.5

QA, KA, VA, OA = 0, NA, 2 * NA, 3 * NA
GI = 4 * NA
GF = GI + HA
QB = GF + HA
KB, VB = QB + NB, QB + 2 * NB
QC = QB + 3 * NB
KC, VC = QC + NC, QC + 2 * NC
COLS = VC + NC
NATC = QC
BLOCKS = [(QA, VA), (VA, GI), (GI, KB), (KB, VB), (VB, QC), (QC, KC), (KC, VC), (VC, COLS)]
GA, GC, GB = 0, 4, 10
GROUPS = 16


class Mem:

    def __init__(self, nc, ctx, phase):
        self.nc, self.ctx, self.phase = nc, ctx, phase
        self.sems = []
        ctx.callback(self.clear)

    def sb(self, name, shape, dt=F32):
        return self.ctx.enter_context(self.nc.sbuf_tensor(f"{self.phase}_{name}", shape, dt))

    def ps(self, name, shape):
        return self.ctx.enter_context(self.nc.psum_tensor(f"{self.phase}_{name}", shape, F32))

    def sem(self, name):
        self.sems.append(self.nc.alloc_semaphore(f"{self.phase}_{name}"))
        return self.sems[-1]

    def clear(self):
        self.nc.clear_and_free_semaphores(self.sems)
        self.nc.all_engine_barrier()


def wait_apart(eng, sem, value, passed):
    eng.wait_ge(sem, value)
    eng.sem_inc(passed, 1)


def row_bcast(vec, n):
    return vec.rearrange("(a d) -> a d", a=1).broadcast_to([n, vec.shape[0]])


def project_phase(nc, A, S, O):
    with ExitStack() as ctx:
        m = Mem(nc, ctx, "p1")
        W = m.sb("W", [P, KD, COLS])
        g_pre = m.sb("g_pre", [P, KD])
        ident = m.sb("ident", [P, P])
        X = [m.sb(f"X{i}", [P, D]) for i in range(2)]
        XN = [m.sb(f"XN{i}", [P, D]) for i in range(2)]
        HT = [m.sb(f"HT{i}", [P, KD, P]) for i in range(2)]
        PT = [m.sb(f"PT{i}", [P, COLS]) for i in range(2)]
        QK = m.sb("QK", [P, GROUPS, P])
        sq = m.sb("sq", [P, D])
        ss = [m.sb(f"ss{i}", [P, 1]) for i in range(2)]
        rs = [m.sb(f"rs{i}", [P, 2]) for i in range(2)]
        eps = m.sb("eps", [P, 1])
        HP = m.ps("HP", [P, 2, 512])
        PP = [m.ps(f"PP{i}", [P, 512]) for i in range(4)]
        QP = [m.ps(f"QP{i}", [P, 4, P]) for i in range(2)]
        w_in = [m.sem(f"w_in{k}") for k in range(KD)]
        g_in = m.sem("g_in")
        passed = m.sem("passed")
        ident_ok = m.sem("ident_ok")
        x_in = [m.sem(f"x_in{i}") for i in range(2)]
        ss_ok = m.sem("ss_ok")
        eps_ok = m.sem("eps_ok")
        ms_ok = m.sem("ms_ok")
        rs_ok = m.sem("rs_ok")
        xn_ok = m.sem("xn_ok")
        turned = m.sem("turned")
        ht_ok = m.sem("ht_ok")
        mm_ok = m.sem("mm_ok")
        blk_ok = m.sem("blk_ok")
        qk_ps = m.sem("qk_ps")
        qk_ok = m.sem("qk_ok")
        nat_out = m.sem("nat_out")
        nat_free = m.sem("nat_free")
        qk_out = m.sem("qk_out")
        qk_free = m.sem("qk_free")

        turn_prompt = {0: (QA, 4, GA), 5: (QC, 3, GC), 6: (KC, 3, GC + 3)}
        turn_sample = {**turn_prompt, 2: (QB, 3, GB), 3: (KB, 3, GB + 3)}
        PER, LAST = len(turn_prompt), NT

        block = ctx.enter_context(nc.Block())
        stores = [("nat", 0, NATC), ("wk", KB, VB), ("wv", VB, QC), ("sk", KC, VC), ("sv", VC, COLS)]

        def store(eng, t, s):
            rows = bass.ds(eng.snap(t * P), P)
            wait_apart(eng, blk_ok, 8 * t + 8 + 4, passed)
            for name, a, b in stores:
                dst = S["nat"] if name == "nat" else O["p_" + name]
                eng.dma_start(dst[rows, :], PT[s][:, a:b]).then_inc(nat_out, 16)
            wait_apart(eng, qk_ok, PER * t + PER + 2, passed)
            eng.dma_start(S["qkT"][0:GB, :, rows].rearrange("g p t -> p g t"), QK[:, 0:GB, :]).then_inc(qk_out, 16)

        def freed(eng, t):
            eng.wait_ge(qk_out, 16 * t + 16)
            eng.sem_inc(qk_free, 1)
            eng.wait_ge(nat_out, 16 * len(stores) * t + 16 * len(stores))
            eng.sem_inc(nat_free, 1)

        @block.sync
        def _(sp):
            sp.dma_start(g_pre[:, :], A["g_pre_mix"].rearrange("(k p) -> p k", p=P), allow_slow_non_contiguous=True).then_inc(g_in, 16)
            for t in range(2):
                sp.dma_start(X[t][:, :], A["x_prompt"][t * P:(t + 1) * P, :]).then_inc(x_in[t], 16)
                if t == 0:
                    for k in range(KD):
                        sp.dma_start(W[:, k, :], A["w_in"][k * P:(k + 1) * P, :]).then_inc(w_in[k], 16)

            def step(t, s, more):
                if more:
                    wait_apart(sp, xn_ok, t + 1, passed)
                    sp.dma_start(X[s][:, :], A["x_prompt"][bass.ds((t + 2) * P, P), :]).then_inc(x_in[s], 16)
                store(sp, t, s)
                freed(sp, t)

            with sp.Fori(0, NT // 2 - 1) as i:
                for s in range(2):
                    step(i * 2 + s, s, True)
            sp.wait_ge(xn_ok, NT - 1)
            for half in range(2):
                sp.dma_start(X[0][half * NS:(half + 1) * NS, :], A["x_sample"][:, :]).then_inc(x_in[0], 16)
            step(NT - 2, 0, False)
            step(NT - 1, 1, False)
            sp.wait_ge(blk_ok, 8 * NT + 8 + 4)
            sp.dma_start(S["nat"][SEQ:TP, :], PT[0][:, 0:NATC]).then_inc(nat_out, 16)
            for name, a, b in stores[3:]:
                sp.dma_start(O["s_" + name][:, :], PT[0][0:NS, a:b]).then_inc(nat_out, 16)
            for name, a, b in stores[1:3]:
                for q in range(DB):
                    sp.dma_start(O["s_" + name][q, WIN - DT:WIN, :], PT[0][q * DT:(q + 1) * DT, a:b]).then_inc(nat_out, 16)
            sp.wait_ge(qk_ok, PER * NT + len(turn_sample) + 2)
            sp.dma_start(S["qkT"][:, :, SEQ:TP].rearrange("g p t -> p g t"), QK[:, :, :]).then_inc(qk_out, 16)
            sp.wait_ge(nat_out, 16 * len(stores) * NT + 16 * (3 + 2 * DB))
            sp.wait_ge(qk_out, 16 * NT + 16)

        @block.gpsimd
        def _(pool):
            pool.memset(eps[:, :], EPS).then_inc(eps_ok, 1)
            pool.memset(ident[:, :], 0.0).then_inc(ident_ok, 1)
            pool.wait_ge(ident_ok, 1)
            pool.affine_select(out=ident[:, :], in_=ident[:, :], compare_op=ALU.not_equal, fill=1.0, base=0,
                               pattern=[[-1, P]], channel_multiplier=1).then_inc(ident_ok, 1)

        @block.scalar
        def _(act):
            act.sem_inc(blk_ok, 4)
            act.sem_inc(nat_free, 2)
            act.wait_ge(eps_ok, 1)

            def squares(t, s, extra=0):
                act.wait_ge(x_in[s], (t - s) * 8 + 16 + extra)
                act.activation(sq[:, :], X[s][:, :], ACT.Square, accum_out=ss[s][:, :]).then_inc(ss_ok, 1)
                act.wait_ge(ss_ok, t + 1)
                act.activation(rs[s][:, 0:1], ss[s][:, :], ACT.Sqrt, scale=1.0 / D, bias=eps[:, :]).then_inc(ms_ok, 1)

            def blocks(t, s, part):
                if part == 0:
                    act.wait_ge(nat_free, t + 1)
                for b in (range(0, 5) if part == 0 else range(5, 8)):
                    a, e = BLOCKS[b]
                    act.wait_ge(mm_ok, 8 * t + b + 1)
                    act.activation(PT[s][:, a:e], PP[b % 4][:, 0:e - a], ACT.Copy).then_inc(blk_ok, 1)

            squares(0, 0)
            with act.Fori(0, NT // 2 - 1) as i:
                for s in range(2):
                    t = i * 2 + s
                    blocks(t, s, 0)
                    act.wait_ge(xn_ok, t + 1)
                    squares(t + 1, 1 - s)
                    blocks(t, s, 1)
            for t in (NT - 2, NT - 1):
                blocks(t, t % 2, 0)
                act.wait_ge(xn_ok, t + 1)
                squares(t + 1, (t + 1) % 2, 16 if t + 1 == NT else 0)
                blocks(t, t % 2, 1)
            blocks(NT, 0, 0)
            blocks(NT, 0, 1)

        @block.vector
        def _(dve):
            dve.sem_inc(ht_ok, 1)
            dve.sem_inc(qk_ok, 2)
            dve.sem_inc(qk_free, 1)
            dve.wait_ge(g_in, 16)

            def norm(t, s):
                dve.wait_ge(ms_ok, t + 1)
                dve.reciprocal(rs[s][:, 1:2], rs[s][:, 0:1]).then_inc(rs_ok, 1)
                dve.wait_ge(rs_ok, t + 1)
                dve.wait_ge(turned, t + 1)
                dve.tensor_scalar(XN[s][:, :], X[s][:, :], rs[s][:, 1:2], None, ALU.mult).then_inc(xn_ok, 1)
                dve.wait_ge(turned, t + 3)
                for h in range(2):
                    ins = dve.tensor_tensor(HT[s][:, 4 * h:4 * h + 4, :], HP[:, h, :].rearrange("p (k t) -> p k t", k=4),
                                            g_pre[:, 4 * h:4 * h + 4, None].broadcast_to([P, 4, P]), ALU.mult)
                ins.then_inc(ht_ok, 1)

            def heads(t, turn, only):
                at = {b: n for n, b in enumerate(sorted(turn))}
                for b in sorted(turn):
                    if b not in only:
                        continue
                    if at[b] == 0:
                        dve.wait_ge(qk_free, t + 1)
                    n = PER * t + at[b]
                    _, k, g = turn[b]
                    dve.wait_ge(qk_ps, n + 1)
                    dve.tensor_copy(QK[:, g:g + k, :], QP[parity[b]][:, 0:k, :]).then_inc(qk_ok, 1)

            norm(0, 0)
            with dve.Fori(0, NT // 2) as i:
                for s in range(2):
                    t = i * 2 + s
                    parity = {0: (PER * s) % 2, 5: (PER * s + 1) % 2, 6: (PER * s + 2) % 2}
                    heads(t, turn_prompt, (0,))
                    norm(t + 1, 1 - s)
                    heads(t, turn_prompt, (5, 6))
            parity = {b: n % 2 for n, b in enumerate(sorted(turn_sample))}
            heads(NT, turn_sample, tuple(turn_sample))

        @block.tensor
        def _(pe):
            pe.sem_inc(turned, 2)
            pe.wait_ge(ident_ok, 2)

            def turn_tile(t, s):
                pe.wait_ge(xn_ok, t + 1)
                pe.wait_ge(ht_ok, t + 1)
                for k in range(KD):
                    ins = pe.transpose(HP[:, k // 4, (k % 4) * P:(k % 4 + 1) * P], XN[s][:, k * P:(k + 1) * P], ident[:, :])
                ins.then_inc(turned, 1)

            def project(t, s, turn, more):
                order = sorted(turn)
                for b, (a, e) in enumerate(BLOCKS):
                    if b == 0:
                        pe.wait_ge(ht_ok, t + 2)
                    pe.wait_ge(blk_ok, 8 * t + b + 1)
                    for k in range(KD):
                        ins = pe.matmul(PP[b % 4][:, 0:e - a], HT[s][:, k, :], W[:, k, a:e], start=(k == 0), stop=(k == KD - 1))
                    ins.then_inc(mm_ok, 1)
                    if b - 1 in turn:
                        turn_heads(t, s, turn, order, b - 1)
                    if b == 4 and more:
                        turn_tile(t + 1, 1 - s)

            def turn_heads(t, s, turn, order, b):
                col, k, _ = turn[b]
                n = PER * t + order.index(b)
                pe.wait_ge(blk_ok, 8 * t + b + 1 + 4)
                pe.wait_ge(qk_ok, n + 1)
                for g in range(k):
                    ins = pe.transpose(QP[parity[b]][:, g, :], PT[s][:, col + g * P:col + (g + 1) * P], ident[:, :])
                ins.then_inc(qk_ps, 1)

            turn_tile(0, 0)
            for k in range(KD):
                pe.wait_ge(w_in[k], 16)
            with pe.Fori(0, NT // 2) as i:
                for s in range(2):
                    parity = {0: (PER * s) % 2, 5: (PER * s + 1) % 2, 6: (PER * s + 2) % 2}
                    project(i * 2 + s, s, turn_prompt, True)
            parity = {b: n % 2 for n, b in enumerate(sorted(turn_sample))}
            project(NT, 0, turn_sample, False)


def stick_prompt_phase(nc, A, S, O):
    CH = 512
    units = []
    for c in range(SEQ // CH):
        for k in range(4 * c + 4):
            for h in range(2):
                units.append((c, k, h, max(3 - k, 0) * P))
    U = len(units)
    BL = U // 2
    chunk_last = [max(u for u in range(U) if units[u][0] == c) for c in range(SEQ // CH)]
    chunk_first = [min(u for u in range(U) if units[u][0] == c) for c in range(SEQ // CH)]
    NZ, NL, NA_, NB_, KV = 3, 4, 3, 6, 4
    AV0 = 2 * KV
    with ExitStack() as ctx:
        m = Mem(nc, ctx, "pc")
        QR = m.sb("QR", [P, SEQ])
        QS = m.sb("QS", [P, SEQ])
        KZ = [[m.sb(f"KZ{h}{i}", [P, P]) for i in range(KV)] for h in range(2)]
        VZ = [[m.sb(f"VZ{h}{i}", [P, P]) for i in range(KV)] for h in range(2)]
        E = [m.sb(f"E{i}", [P, CH]) for i in range(NZ)]
        L = [m.sb(f"L{i}", [P, CH]) for i in range(NL)]
        T = [m.sb(f"T{i}", [P, CH]) for i in range(NA_)]
        SL = [[m.sb(f"SL{h}{i}", [P, CH]) for i in range(2)] for h in range(2)]
        YS = [m.sb(f"YS{i}", [P, CH]) for i in range(2)]
        ident = m.sb("ident", [P, P])
        mask = m.sb("mask", [P, P])
        zeros = m.sb("zeros", [P, P])
        ntri = m.sb("ntri", [P, P])
        nones = m.sb("nones", [P, P])
        bsb = m.sb("bsb", [P, HC])
        bh = m.sb("bh", [P, 2])
        ZP = [m.ps(f"ZP{i}", [P, CH]) for i in range(NB_)]
        YP = [m.ps(f"YP{i}", [P, CH]) for i in range(2)]
        consts = m.sem("consts")
        pads = m.sem("pads")
        passed = m.sem("passed")
        b_in = m.sem("b_in")
        q_in = m.sem("q_in")
        kv_in = [m.sem(f"kv_in{i}") for i in range(KV)]
        qs_ok = m.sem("qs_ok")
        bh_ok = m.sem("bh_ok")
        z_ok = m.sem("z_ok")
        zc_ok = m.sem("zc_ok")
        e_ok = m.sem("e_ok")
        sp_ok = m.sem("sp_ok")
        l_ok = m.sem("l_ok")
        s_ok = m.sem("s_ok")
        arg_ok = m.sem("arg_ok")
        a_ok = m.sem("a_ok")
        av_ok = m.sem("av_ok")
        yc_ok = m.sem("yc_ok")
        y_out = [m.sem(f"y_out{i}") for i in range(2)]
        block = ctx.enter_context(nc.Block())

        @block.gpsimd
        def _(pool):
            for s in range(2):
                pool.sem_inc(y_out[s], 16)
            pool.sem_inc(s_ok, NL)
            for t in (ident, mask, zeros):
                pool.memset(t[:, :], 0.0)
            for t in (ntri, nones):
                pool.memset(t[:, :], -1.0)
            pool.memset(bh[:, :], 0.0).then_inc(consts, 1)
            pool.wait_ge(consts, 1)
            pool.affine_select(out=ident[:, :], in_=ident[:, :], compare_op=ALU.not_equal, fill=1.0, base=0,
                               pattern=[[-1, P]], channel_multiplier=1)
            pool.affine_select(out=mask[:, :], in_=mask[:, :], compare_op=ALU.is_gt, fill=NEG, base=0,
                               pattern=[[1, P]], channel_multiplier=-1)
            pool.affine_select(out=ntri[:, :], in_=ntri[:, :], compare_op=ALU.is_ge, fill=0.0, base=0,
                               pattern=[[-1, P]], channel_multiplier=1).then_inc(consts, 1)

            with pool.Fori(0, 3) as g:
                for u, (c, k, h, a) in enumerate(units):
                    pool.wait_ge(l_ok, g * U + u + 1 + NZ)
                    pool.wait_ge(arg_ok, g * U + u - 1 + NL)
                    pool.wait_ge(s_ok, g * U + u - 1 + NL)
                    if k == 0:
                        pool.tensor_tensor(SL[h][1][:, a:CH], L[u % NL][:, a:CH], zeros[:, :], ALU.add).then_inc(s_ok, 1)
                        continue
                    new, old = SL[h][(k + 1) % 2], SL[h][k % 2]
                    if k < 4:
                        pool.tensor_tensor(new[:, a:a + P], L[u % NL][:, a:a + P], zeros[:, :], ALU.add)
                        a += P
                    pool.tensor_tensor(new[:, a:CH], old[:, a:CH], L[u % NL][:, a:CH], ALU.add).then_inc(s_ok, 1)

        @block.sync
        def _(sp):
            sp.dma_start(bsb[:, :], row_bcast(A["b_sb"], P)).then_inc(b_in, 16)
            sp.wait_ge(pads, 1)
            with sp.Fori(0, 3) as g:
                wait_apart(sp, qs_ok, g + 1, passed)
                sp.dma_start(QR[:, :], S["qkT"][bass.ds(g + GC, 1), :, 0:SEQ].rearrange("a p t -> p (a t)")).then_inc(q_in, 16)
                for c in range(SEQ // CH):
                    with sp.Fori(0, c + 1) as n:
                        for i in range(KV):
                            j = n * KV + (2 * c * (c + 1) + i)
                            rows = bass.ds(n * (-KV * P) + (4 * c + 3 - i) * P, P)
                            wait_apart(sp, av_ok, g * U + j * 2 + 2, passed)
                            kT = S["qkT"][bass.ds(g + GC + 3, 1), :, rows].rearrange("a p t -> p (a t)")
                            for h in range(2):
                                half = slice(h * HD, (h + 1) * HD)
                                sp.dma_start(KZ[h][i][half, :], kT[half, :]).then_inc(kv_in[i], 16)
                                sp.dma_start(VZ[h][i][:, half], O["p_sv"][rows, bass.ds(g * P + h * HD, HD)]).then_inc(kv_in[i], 16)

        @block.scalar
        def _(act):
            act.preload_act_table_set("natural_log_exp_and_others")
            act.sem_inc(a_ok, NB_)
            act.wait_ge(consts, 2)

            def weights(g, u):
                c, k, h, a = units[u]
                act.wait_ge(arg_ok, g * U + u + 1 + NL)
                act.wait_ge(av_ok, g * U + u - NA_ + 1 + AV0)
                act.activation(T[u % NA_][:, a:CH], ZP[u % NB_][:, a:CH], ACT.Exp, bias=bh[:, h:h + 1]).then_inc(a_ok, 1)

            def store(g, c):
                act.wait_ge(yc_ok, g * 4 + c + 3)
                act.dma_start(S["yT"][bass.ds(g + 5, 1), :, c * CH:(c + 1) * CH].rearrange("a p t -> p (a t)"), YS[c % 2][:, :]).then_inc(y_out[c % 2], 16)

            with act.Fori(0, 3) as g:
                for v in range(U + 3):
                    if v - 12 in chunk_last:
                        store(g, chunk_last.index(v - 12))
                    if v < U:
                        a, e = units[v][3], E[v % NZ]
                        act.wait_ge(zc_ok, g * U + v + 1)
                        act.activation(e[:, a:CH], e[:, a:CH], ACT.Exp).then_inc(e_ok, 1)
                        act.wait_ge(e_ok, g * U + v + 1)
                        act.activation(e[:, a:CH], e[:, a:CH], ACT.Ln, bias=1.0).then_inc(sp_ok, 1)
                    if v >= 3:
                        weights(g, v - 3)
                store(g, SEQ // CH - 1)
            for s in range(2):
                act.wait_ge(y_out[s], 16 * 7)

        @block.vector
        def _(dve):
            dve.sem_inc(qs_ok, 1)
            dve.sem_inc(l_ok, NZ)
            dve.sem_inc(yc_ok, 2)
            for h in range(2):
                for i in range(KV):
                    dve.memset(KZ[h][i][(1 - h) * HD:(2 - h) * HD, :], 0.0)
                    ins = dve.memset(VZ[h][i][:, (1 - h) * HD:(2 - h) * HD], 0.0)
            ins.then_inc(pads, 1)
            dve.wait_ge(consts, 2)
            dve.wait_ge(b_in, 16)

            def bound(g, u):
                c, k, h, a = units[u]
                dve.wait_ge(z_ok, g * U + u + 2)
                dve.wait_ge(l_ok, g * U + u + 1)
                dve.tensor_scalar(E[u % NZ][:, a:CH], ZP[u % NB_][:, a:CH], bh[:, h:h + 1], 40.0, ALU.add, ALU.min).then_inc(zc_ok, 1)

            def softplus(g, u):
                c, k, h, a = units[u]
                dve.wait_ge(sp_ok, g * U + u + 1)
                dve.wait_ge(arg_ok, g * U + u + 1)
                dve.wait_ge(s_ok, g * U + u + 1)
                dve.scalar_tensor_tensor(out=L[u % NL][:, a:CH], in0=ZP[u % NB_][:, a:CH], scalar=bh[:, h:h + 1],
                                         in1=E[u % NZ][:, a:CH], op0=ALU.add, op1=ALU.max).then_inc(l_ok, 1)

            def output(g, c):
                dve.wait_ge(av_ok, g * U + chunk_last[c] + 1 + AV0)
                dve.wait_ge(y_out[c % 2], (g * 2 + c // 2) * 16 + 16)
                dve.tensor_copy(YS[c % 2][:, :], YP[c % 2][:, :]).then_inc(yc_ok, 1)

            with dve.Fori(0, 3) as g:
                dve.wait_ge(q_in, g * 16 + 16)
                dve.wait_ge(z_ok, g * U + 1)
                dve.tensor_scalar(QS[:, :], QR[:, :], SCALE, None, ALU.mult).then_inc(qs_ok, 1)
                dve.wait_ge(a_ok, g * U + NB_)
                dve.tensor_copy(bh[:, :], bsb[:, bass.ds(g * 2, 2)]).then_inc(bh_ok, 1)
                dve.wait_ge(bh_ok, g + 1)
                for v in range(U + 1):
                    if v < U:
                        bound(g, v)
                    if v >= 1:
                        softplus(g, v - 1)
                    if v - 8 in chunk_last:
                        output(g, chunk_last.index(v - 8))
                output(g, SEQ // CH - 1)

        @block.tensor
        def _(pe):
            pe.sem_inc(z_ok, 1)
            pe.sem_inc(arg_ok, NL)
            pe.sem_inc(av_ok, AV0)
            pe.wait_ge(consts, 2)
            pe.wait_ge(pads, 1)

            def logits(g, u):
                c, k, h, a = units[u]
                i = (u // 2) % KV
                if h == 0:
                    pe.wait_ge(kv_in[i], (g * (BL // KV) + u // 2 // KV) * 64 + 64)
                pe.wait_ge(a_ok, g * U + u + 1)
                ins = pe.matmul(ZP[u % NB_][:, a:CH], KZ[h][i][:, :], QS[:, c * CH + a:(c + 1) * CH], start=True, stop=True)
                if k < 4:
                    ins = pe.matmul(ZP[u % NB_][:, a:a + P], ident[:, :], mask[:, :], start=False, stop=True, skip_group_check=True)
                ins.then_inc(z_ok, 1)

            def exponents(g, u):
                c, k, h, a = units[u]
                pe.wait_ge(l_ok, g * U + u + 1 + NZ)
                ins = pe.matmul(ZP[u % NB_][:, a:CH], ntri[:, :], L[u % NL][:, a:CH], start=False, stop=True, skip_group_check=True)
                if k > 0:
                    b = a + P if k < 4 else a
                    pe.wait_ge(s_ok, g * U + u - 1 + NL)
                    ins = pe.matmul(ZP[u % NB_][:, b:CH], nones[:, :], SL[h][k % 2][:, b:CH], start=False, stop=True, skip_group_check=True)
                ins.then_inc(arg_ok, 1)

            def values(g, u):
                c, k, h, a = units[u]
                if u == chunk_first[c]:
                    pe.wait_ge(yc_ok, g * 4 + c + 1)
                pe.wait_ge(a_ok, g * U + u + 1 + NB_)
                pe.matmul(YP[c % 2][:, a:CH], VZ[h][(u // 2) % KV][:, :], T[u % NA_][:, a:CH], start=(u == chunk_first[c]),
                          stop=(u == chunk_last[c]), skip_group_check=True).then_inc(av_ok, 1)

            with pe.Fori(0, 3) as g:
                for v in range(-3, U + 2):
                    if v == -3:
                        pe.wait_ge(qs_ok, g + 2)
                    if v + 3 < U:
                        logits(g, v + 3)
                    if 0 <= v < U:
                        exponents(g, v)
                    if v >= 2:
                        values(g, v - 2)


def dilated_prompt_phase(nc, A, S, O):
    OUTW = NB + 2 * HB
    nat = S["nat"][0:SEQ, QB:QC]
    views = [nat.rearrange("(n i) c -> n i c", i=P),
             nat.rearrange("(n i r) c -> n r i c", i=P, r=4),
             nat.rearrange("(i r) c -> r i c", r=16)]
    outs = [S["br"][0].rearrange("(n i) c -> n i c", i=P),
            S["br"][1].rearrange("(n i r) c -> n r i c", i=P, r=4),
            S["br"][2].rearrange("(i r) c -> r i c", r=16)]

    def flat(ap):
        return ap.rearrange("a i c -> i (a c)")

    def b1(v, n):
        return flat(v[0][bass.ds(n, 1)])

    def b2(v, n, r):
        return flat(v[1][n, bass.ds(r, 1)])

    def b3(v, r):
        return flat(v[2][bass.ds(r, 1)])

    NO, PREV = [False] * 4, [False] + [True] * 3
    bodies = [(1, 0, PREV, lambda v, i, q: b1(v, q), None),
              (3, 4, [True] * 4, lambda v, i, q: b1(v, i * 4 + 4 + q), True),
              (4, 16, PREV, lambda v, i, q: b2(v, q, i), True),
              (1, 32, NO, lambda v, i, q: b3(v, q), True),
              (3, 36, NO, lambda v, i, q: b3(v, i * 4 + 4 + q), False)]

    def each(eng, step):
        for trips, first, prev, rows, before in bodies:
            if trips == 1:
                for q in range(4):
                    step(first + q, q, prev[q], lambda v, q=q: rows(v, 0, q), prev[q - 1] if q else before)
                continue
            with eng.Fori(0, trips) as i:
                for q in range(4):
                    step(i * 4 + (first + q), q, prev[q], lambda v, q=q: rows(v, i, q), prev[q - 1] if q else before)

    with ExitStack() as ctx:
        m = Mem(nc, ctx, "pb")
        X = [m.sb(f"X{i}", [P, 3, HB // 2, P]) for i in range(4)]
        QT = [m.sb(f"QT{i}", [P, 3, P]) for i in range(2)]
        KT = [m.sb(f"KT{i}", [P, 2, 3, P]) for i in range(4)]
        SM = [m.sb(f"SM{i}", [P, HB, 256]) for i in range(2)]
        PR = [m.sb(f"PR{i}", [P, HB, 256]) for i in range(2)]
        PT = [m.sb(f"PT{i}", [P, 3, 4, P]) for i in range(2)]
        OT = [m.sb(f"OT{i}", [P, OUTW]) for i in range(2)]
        nm = [m.sb(f"nm{i}", [P, HB]) for i in range(2)]
        mask = m.sb("mask", [P, 256])
        ident = m.sb("ident", [P, P])
        TP_ = m.ps("TP", [P, 2, 512])
        SP = [m.ps(f"SP{i}", [P, 3, 512]) for i in range(2)]
        consts = m.sem("consts")
        zero_ok = m.sem("zero_ok")
        passed, passed_dve, passed_pool = m.sem("passed"), m.sem("passed_dve"), m.sem("passed_pool")
        x_in = [m.sem(f"x_in{i}") for i in range(4)]
        t_ok = m.sem("t_ok")
        qt_ok = m.sem("qt_ok")
        kt_ok = m.sem("kt_ok")
        s_ok = m.sem("s_ok")
        mx_ok = m.sem("mx_ok")
        nm_ok = m.sem("nm_ok")
        p_ok = m.sem("p_ok")
        pt_ok = m.sem("pt_ok")
        pa_ok = m.sem("pa_ok")
        pb_ok = m.sem("pb_ok")
        pv_ok = m.sem("pv_ok")
        o_ok = m.sem("o_ok")
        o_out = m.sem("o_out")
        o_free = m.sem("o_free")
        block = ctx.enter_context(nc.Block())

        @block.gpsimd
        def _(pool):
            pool.sem_inc(o_free, 2)
            pool.memset(ident[:, :], 0.0)
            pool.memset(mask[:, :], 0.0).then_inc(consts, 1)
            pool.wait_ge(consts, 1)
            pool.affine_select(out=ident[:, :], in_=ident[:, :], compare_op=ALU.not_equal, fill=1.0, base=0,
                               pattern=[[-1, P]], channel_multiplier=1).then_inc(consts, 1)
            pool.affine_select(out=mask[:, 0:P], in_=mask[:, 0:P], compare_op=ALU.is_ge, fill=NEG, base=0,
                               pattern=[[1, P]], channel_multiplier=-1).then_inc(consts, 1)
            pool.affine_select(out=mask[:, P:256], in_=mask[:, P:256], compare_op=ALU.is_ge, fill=NEG, base=0,
                               pattern=[[-1, P]], channel_multiplier=1).then_inc(consts, 1)

            def step(u, q, prev, rows, before):
                wait_apart(pool, o_ok, u + 3, passed_pool)
                pool.dma_start(rows(outs), OT[q % 2][:, :]).then_inc(o_out, 16)
                pool.wait_ge(o_out, u * 16 + 16)
                pool.sem_inc(o_free, 1)

            each(pool, step)

        @block.sync
        def _(sp):
            def step(u, q, prev, rows, before):
                wait_apart(sp, pv_ok, u + 2, passed)
                sp.dma_start(X[q][:, :, :, :].rearrange("p a g c -> p (a g c)"), rows(views)).then_inc(x_in[q], 16)


            each(sp, step)

        @block.scalar
        def _(act):
            act.preload_act_table_set("natural_log_exp_and_others")
            act.sem_inc(qt_ok, 1)
            act.wait_ge(consts, 4)

            def turned(u, q, prev):
                act.wait_ge(pt_ok, u * 3 + 1)
                a = 0 if prev else 2
                w = PT[q % 2][:, 0, 0:4 - a, :]
                act.activation(w, SP[q % 2][:, 0, 0:(4 - a) * P].rearrange("p (n c) -> p n c", c=P), ACT.Copy).then_inc(pa_ok, 1)

            def step(u, q, prev, rows, before):
                act.wait_ge(t_ok, u + 1)
                act.activation(QT[q % 2][:, :, :], TP_[:, 0, 0:3 * P].rearrange("p (g c) -> p g c", c=P), ACT.Copy,
                               scale=SCALE).then_inc(qt_ok, 1)
                if before is not None or q > 0:
                    turned(u - 1, q - 1, before)
                a = 0 if prev else P
                for h in range(HB):
                    act.wait_ge(nm_ok, (u * HB + h // 2 * 2) + 2)
                    act.activation(PR[q % 2][:, h, a:256], SM[q % 2][:, h, a:256], ACT.Exp, bias=nm[q % 2][:, h:h + 1],
                                   accum_out=OT[q % 2][:, NB + HB + h:NB + HB + h + 1]).then_inc(p_ok, 1)

            each(act, step)
            turned(47, 3, False)

        @block.vector
        def _(dve):
            dve.sem_inc(kt_ok, 1)
            dve.sem_inc(o_ok, 2)
            for q in range(4):
                for h in range(2):
                    ins = dve.memset(KT[q][(1 - h) * HD:(2 - h) * HD, h, :, :], 0.0)
            ins.then_inc(zero_ok, 1)
            dve.wait_ge(consts, 4)

            def turned(u, q, prev):
                n = 4 if prev else 2
                dve.wait_ge(pt_ok, u * 3 + 3)
                dve.tensor_copy(PT[q % 2][:, 1:3, 0:n, :], SP[q % 2][:, 1:3, 0:n * P].rearrange("p b (n c) -> p b n c", c=P)).then_inc(pb_ok, 1)

            def output(u, q):
                dve.wait_ge(pv_ok, u + 1 + 4)
                dve.tensor_copy(OT[q % 2][:, 0:NB], SP[q % 2][:, 0, 0:NB]).then_inc(o_ok, 1)

            def step(u, q, prev, rows, before):
                dve.wait_ge(t_ok, u + 1)
                for h in range(2):
                    half = slice(h * HD, (h + 1) * HD)
                    ins = dve.tensor_copy(KT[q][half, h, :, :], TP_[half, 1, 0:3 * P].rearrange("p (g c) -> p g c", c=P))
                ins.then_inc(kt_ok, 1)
                if before is not None or q > 0:
                    turned(u - 1, q - 1, before)
                wait_apart(dve, s_ok, u + 1, passed_dve)
                wait_apart(dve, o_free, u + 1, passed_dve)
                a = 0 if prev else P
                for h in range(HB):
                    dve.tensor_tensor_reduce(out=SM[q % 2][:, h, a:256], in0=SP[q % 2][:, h // 2, h % 2 * 256 + a:h % 2 * 256 + 256],
                                             in1=mask[:, a:256], scale=1.0, scalar=-3e38, op0=ALU.add, op1=ALU.max,
                                             accum_out=OT[q % 2][:, NB + h:NB + h + 1]).then_inc(mx_ok, 1)
                    if h % 2:
                        dve.wait_ge(mx_ok, u * HB + h + 1)
                        dve.tensor_scalar(nm[q % 2][:, h - 1:h + 1], OT[q % 2][:, NB + h - 1:NB + h + 1], -1.0, None, ALU.mult).then_inc(nm_ok, 2)
                if before is not None or q > 0:
                    output(u - 1, q - 1)

            each(dve, step)
            turned(47, 3, False)
            output(47, 3)

        @block.tensor
        def _(pe):
            pe.sem_inc(pv_ok, 4)
            pe.wait_ge(consts, 4)
            pe.wait_ge(zero_ok, 1)

            def turn_p(u, q, prev):
                n = 2 if prev else 1
                for b in range(3):
                    pe.wait_ge(p_ok, u * HB + 2 * b + 2)
                    for h in range(2):
                        for k in range(n):
                            ins = pe.transpose(SP[q % 2][:, b, (h * n + k) * P:(h * n + k + 1) * P],
                                               PR[q % 2][:, 2 * b + h, (2 - n + k) * P:(3 - n + k) * P], ident[:, :])
                    ins.then_inc(pt_ok, 1)

            def values(u, q, prev):
                n = 2 if prev else 1
                pe.wait_ge(pa_ok, u + 1)
                pe.wait_ge(pb_ok, u + 1)
                for h in range(HB):
                    for k in range(n):
                        slot = (q - 1) % 4 if n == 2 and k == 0 else q
                        ins = pe.matmul(SP[q % 2][:, 0, h * HD:(h + 1) * HD], PT[q % 2][:, h // 2, (h % 2) * n + k, :],
                                        X[slot][:, 2, h // 2, h % 2 * HD:(h % 2 + 1) * HD], start=(k == 0), stop=(k == n - 1))
                ins.then_inc(pv_ok, 1)

            def step(u, q, prev, rows, before):
                pe.wait_ge(x_in[q], (u - q) * 4 + 16)
                pe.wait_ge(qt_ok, u + 1)
                pe.wait_ge(kt_ok, u + 1)
                for a in range(2):
                    for g in range(3):
                        ins = pe.transpose(TP_[:, a, g * P:(g + 1) * P], X[q][:, a, g, :], ident[:, :])
                ins.then_inc(t_ok, 1)
                if before is not None or q > 0:
                    turn_p(u - 1, (q - 1) % 4, before)
                pe.wait_ge(qt_ok, u + 2)
                pe.wait_ge(kt_ok, u + 2)
                pe.wait_ge(o_ok, u + 1)
                for h in range(HB):
                    for k in range(0 if prev else 1, 2):
                        slot = (q - 1) % 4 if k == 0 else q
                        ins = pe.matmul(SP[q % 2][:, h // 2, h % 2 * 256 + k * P:h % 2 * 256 + (k + 1) * P],
                                        QT[q % 2][:, h // 2, :], KT[slot][:, h % 2, h // 2, :], start=True, stop=True)
                ins.then_inc(s_ok, 1)
                if before is not None or q > 0:
                    values(u - 1, (q - 1) % 4, before)

            each(pe, step)
            turn_p(47, 3, False)
            values(47, 3, False)


def dilated_merge_phase(nc, A, S, O):
    W = NB + 2 * HB
    G0 = NA // P
    with ExitStack() as ctx:
        m = Mem(nc, ctx, "pm")
        R = [m.sb(f"R{i}", [P, 3, W]) for i in range(2)]
        mx = [m.sb(f"mx{i}", [P, 2, HB]) for i in range(2)]
        w = [m.sb(f"w{i}", [P, 3, HB]) for i in range(2)]
        wd = [m.sb(f"wd{i}", [P, 3, HB]) for i in range(2)]
        den = [m.sb(f"den{i}", [P, 3, HB]) for i in range(2)]
        T = [m.sb(f"T{i}", [P, 3, NB]) for i in range(2)]
        Y = [m.sb(f"Y{i}", [P, NB]) for i in range(2)]
        YT = [m.sb(f"YT{i}", [P, 3, P]) for i in range(2)]
        ident = m.sb("ident", [P, P])
        YP = m.ps("YP", [P, 3, P])
        consts = m.sem("consts")
        passed = m.sem("passed")
        r_in = [m.sem(f"r_in{i}") for i in range(2)]
        wa_ok = m.sem("wa_ok")
        w_ok = m.sem("w_ok")
        dv = m.sem("dv")
        yt_ok = m.sem("yt_ok")
        yc_ok = m.sem("yc_ok")
        y_out = [m.sem(f"y_out{i}") for i in range(2)]
        block = ctx.enter_context(nc.Block())
        STEPS = 11

        @block.gpsimd
        def _(pool):
            for s in range(2):
                pool.sem_inc(y_out[s], 16)
            pool.memset(ident[:, :], 0.0).then_inc(consts, 1)
            pool.wait_ge(consts, 1)
            pool.affine_select(out=ident[:, :], in_=ident[:, :], compare_op=ALU.not_equal, fill=1.0, base=0,
                               pattern=[[-1, P]], channel_multiplier=1).then_inc(consts, 1)

        @block.sync
        def _(sp):
            def load(t, s):
                sp.dma_start(R[s][:, :, :], S["br"][:, bass.ds(t * P, P), :].rearrange("b p c -> p b c")).then_inc(r_in[s], 16)

            load(0, 0)
            load(1, 1)
            with sp.Fori(1, NT // 2) as i:
                for s in range(2):
                    wait_apart(sp, dv, (i * 2 + s - 1) * STEPS, passed)
                    load(i * 2 + s, s)

        @block.scalar
        def _(act):
            with act.Fori(0, NT // 2) as i:
                for s in range(2):
                    t = i * 2 + s
                    act.wait_ge(wa_ok, t + 1)
                    act.activation(w[s][:, :, :], w[s][:, :, :], ACT.Exp).then_inc(w_ok, 1)
                    act.wait_ge(yc_ok, t + 2)
                    act.dma_start(S["yT"][G0:G0 + 3, :, bass.ds(t * P, P)].rearrange("g p t -> p g t"), YT[s][:, :, :]).then_inc(y_out[s], 16)
            for s in range(2):
                act.wait_ge(y_out[s], 16 * (NT // 2 + 1))

        @block.vector
        def _(dve):
            dve.sem_inc(yc_ok, 1)

            def bc(x):
                return x[:, :, :, None].broadcast_to([P, 3, HB, HD])

            with dve.Fori(0, NT // 2) as i:
                for s in range(2):
                    t = i * 2 + s
                    n = [0]

                    def then(ins, base=t * STEPS):
                        n[0] += 1
                        ins.then_inc(dv, 1)
                        dve.wait_ge(dv, base + n[0])

                    dve.wait_ge(r_in[s], i * 16 + 16)
                    mxs, dens = R[s][:, :, NB:NB + HB], R[s][:, :, NB + HB:W]
                    then(dve.tensor_tensor(mx[s][:, 0, :], mxs[:, 0, :], mxs[:, 1, :], ALU.max))
                    then(dve.tensor_tensor(mx[s][:, 1, :], mx[s][:, 0, :], mxs[:, 2, :], ALU.max))
                    dve.tensor_tensor(w[s][:, :, :], mxs, mx[s][:, 1:2, :].broadcast_to([P, 3, HB]), ALU.subtract).then_inc(wa_ok, 1)
                    dve.wait_ge(w_ok, t + 1)
                    then(dve.tensor_tensor(wd[s][:, :, :], w[s][:, :, :], dens, ALU.mult))
                    then(dve.tensor_tensor(den[s][:, 0, :], wd[s][:, 0, :], wd[s][:, 1, :], ALU.add))
                    then(dve.tensor_tensor(den[s][:, 1, :], den[s][:, 0, :], wd[s][:, 2, :], ALU.add))
                    then(dve.reciprocal(den[s][:, 2, :], den[s][:, 1, :]))
                    then(dve.tensor_tensor(w[s][:, :, :], w[s][:, :, :], den[s][:, 2:3, :].broadcast_to([P, 3, HB]), ALU.mult))
                    then(dve.tensor_tensor(T[s][:, :, :].rearrange("p b (h e) -> p b h e", e=HD),
                                           R[s][:, :, 0:NB].rearrange("p b (h e) -> p b h e", e=HD), bc(w[s]), ALU.mult))
                    then(dve.tensor_tensor(Y[s][:, :], T[s][:, 0, :], T[s][:, 1, :], ALU.add))
                    then(dve.tensor_tensor(Y[s][:, :], Y[s][:, :], T[s][:, 2, :], ALU.add))
                    dve.wait_ge(yt_ok, t + 1)
                    dve.wait_ge(y_out[s], i * 16 + 16)
                    dve.tensor_copy(YT[s][:, :, :], YP[:, :, :]).then_inc(yc_ok, 1)
                    n[0] += 1
                    dve.sem_inc(dv, 1)

        @block.tensor
        def _(pe):
            pe.wait_ge(consts, 2)
            with pe.Fori(0, NT // 2) as i:
                for s in range(2):
                    t = i * 2 + s
                    pe.wait_ge(dv, t * STEPS + 10)
                    pe.wait_ge(yc_ok, t + 1)
                    for g in range(3):
                        ins = pe.transpose(YP[:, g, :], Y[s][:, g * P:(g + 1) * P], ident[:, :])
                    ins.then_inc(yt_ok, 1)


def mlstm_chunks(nc, A, S, O, sample):
    R = NS if sample else P
    E1 = HD + 1
    with ExitStack() as ctx:
        m = Mem(nc, ctx, "ms" if sample else "mp")
        X = [m.sb(f"X{i}", [P, QB]) for i in range(2)]
        QT = [m.sb(f"QT{i}", [P, 2, R]) for i in range(2)]
        KZ = [m.sb(f"KZ{i}", [P, 2, 2, R]) for i in range(2)]
        bias = m.sb("bias", [P, 2 * HA])
        gm = m.sb("gm", [P, NA])
        eps = m.sb("eps", [P, 1])
        ident, tri, ones, last = (m.sb(x, [P, P]) for x in ("ident", "tri", "ones", "last"))
        mask = m.sb("mask", [P, P])
        VX = m.sb("VX", [P, HA, E1])
        CT = m.sb("CT", [P, DB if sample else 1, HA, E1])
        mr = m.sb("mr", [P, HA])
        f, nf, sp_, lf, ig, bb, aa, am, gg, ng, ex, mt, dn, r1, rs = (
            m.sb(x, [P, HA]) for x in ("f", "nf", "sp", "lf", "ig", "bb", "aa", "am", "gg", "ng", "ex", "mt", "dn", "r1", "rs"))
        GM = m.sb("GM", [P, 2 * HA])
        EX = m.sb("EX", [P, 2, HA])
        EE = m.sb("EE", [P, 2, HA])
        DA = m.sb("DA", [P, HA, R])
        AM = m.sb("AM", [P, HA, R])
        DD = m.sb("DD", [P, HA, R])
        SD = m.sb("SD", [P, HA, R])
        ST = m.sb("ST", [P, HA, R])
        NU = m.sb("NU", [P, HA, E1])
        HH = m.sb("HH", [P, HA, HD])
        HS = m.sb("HS", [P, HA, HD])
        OG = m.sb("OG", [P, NA])
        YY = m.sb("YY", [P, HA, HD])
        YT = m.sb("YT", [P, 2, R])
        KW = m.sb("KW", [P, HA, HD])
        UC = m.sb("UC", [P, HA, P])
        pA = m.ps("pA", [P, HA, P])
        pS = m.ps("pS", [P, HA, P])
        pI = m.ps("pI", [P, HA, E1])
        pQ = m.ps("pQ", [P, HA, E1])
        pB = m.ps("pB", [P, 512])
        pU = m.ps("pU", [P, HA, P])
        if sample:
            C0 = m.sb("C0", [E1, DB, HA, HD])
            blk = m.sb("blk", [P, DB])
            blast = m.sb("blast", [P, DB])
            bcol = m.sb("bcol", [P, DB, NS])
            QM = m.sb("QM", [P, 2, DB, NS])
            VM = m.sb("VM", [NS, DB, HA, E1])
            DS = m.sb("DS", [NS, DB, HA])
            C1 = m.sb("C1", [E1, DB, HA, HD])
            pC = m.ps("pC", [P, 2, 512])
        names = ["consts", "w_in", "ready", "f", "nf", "ex", "sp", "lf", "b", "bc", "a", "da", "ab", "am", "g", "gm", "wx",
                 "wex", "lastr", "ee", "eex", "dec", "s", "sd", "st", "stc", "intra", "inter", "num", "num2", "den", "den2",
                 "rden", "h", "hsq", "ssq", "ln", "rsq", "og", "og1", "og2", "y1", "y2", "y3", "yt", "vx", "kw", "up", "ct", "done",
                 "tail", "tailv", "vm", "ngs", "zero", "blkm", "drain"]
        ok = {x: m.sem(x + "_ok") for x in names}
        x_in = [m.sem(f"x_in{i}") for i in range(2)]
        passed, passed_dve = m.sem("passed"), m.sem("passed_dve")
        y_out = m.sem("y_out")
        o_out = m.sem("o_out")
        block = ctx.enter_context(nc.Block())
        row0 = SEQ if sample else 0

        def chunks(eng, chunk):
            if sample:
                chunk(0, 0)
                return
            with eng.Fori(0, NT // 2) as i:
                for s in range(2):
                    chunk(i * 2 + s, s)

        def bc(x, n):
            return x[:, :, None].broadcast_to([R, HA, n])

        @block.gpsimd
        def _(pool):
            c = [0]

            def then(ins):
                c[0] += 1
                ins.then_inc(ok["consts"], 1)
                pool.wait_ge(ok["consts"], c[0])

            then(pool.memset(eps[:, :], EPS))
            then(pool.memset(ident[:, :], 0.0))
            then(pool.affine_select(out=ident[:, :], in_=ident[:, :], compare_op=ALU.not_equal, fill=1.0, base=0,
                                    pattern=[[-1, P]], channel_multiplier=1))
            then(pool.memset(ones[:, :], 1.0))
            then(pool.memset(tri[:, :], 1.0))
            then(pool.memset(mask[:, :], 0.0))
            then(pool.memset(last[:, :], 1.0))
            then(pool.affine_select(out=tri[:, :], in_=tri[:, :], compare_op=ALU.is_ge, fill=0.0, base=0,
                                    pattern=[[1, P]], channel_multiplier=-1))
            then(pool.affine_select(out=mask[:, :], in_=mask[:, :], compare_op=ALU.is_ge, fill=NEG, base=0,
                                    pattern=[[-1, P]], channel_multiplier=1))
            if not sample:
                then(pool.affine_select(out=last[:, :], in_=last[:, :], compare_op=ALU.is_ge, fill=0.0, base=-(P - 1),
                                        pattern=[[0, P]], channel_multiplier=1))
            else:
                n = P // DT
                v = lambda x: x[:, :].rearrange("p (b t) -> p b t", t=DT)
                then(pool.affine_select(out=v(tri), in_=v(tri), compare_op=ALU.is_ge, fill=0.0, base=0,
                                        pattern=[[-DT, n], [0, DT]], channel_multiplier=1))
                then(pool.affine_select(out=v(mask), in_=v(mask), compare_op=ALU.is_ge, fill=NEG, base=DT - 1,
                                        pattern=[[DT, n], [0, DT]], channel_multiplier=-1))
                then(pool.affine_select(out=v(last), in_=v(last), compare_op=ALU.is_equal, fill=0.0, base=-(DT - 1),
                                        pattern=[[-DT, n], [0, DT]], channel_multiplier=1))
                then(pool.memset(blk[:, :], 1.0))
                then(pool.memset(blast[:, :], 1.0))
                then(pool.memset(bcol[:, :, :], 1.0))
                then(pool.affine_select(out=blk[:, :], in_=blk[:, :], compare_op=ALU.is_ge, fill=0.0, base=0,
                                        pattern=[[-DT, DB]], channel_multiplier=1))
                then(pool.affine_select(out=blk[:, :], in_=blk[:, :], compare_op=ALU.is_ge, fill=0.0, base=DT - 1,
                                        pattern=[[DT, DB]], channel_multiplier=-1))
                then(pool.affine_select(out=blast[:, :], in_=blast[:, :], compare_op=ALU.is_equal, fill=0.0, base=-(DT - 1),
                                        pattern=[[-DT, DB]], channel_multiplier=1))
                then(pool.affine_select(out=bcol[:, :, :], in_=bcol[:, :, :], compare_op=ALU.is_ge, fill=0.0, base=0,
                                        pattern=[[-DT, DB], [1, NS]], channel_multiplier=0))
                then(pool.affine_select(out=bcol[:, :, :], in_=bcol[:, :, :], compare_op=ALU.is_ge, fill=0.0, base=DT - 1,
                                        pattern=[[DT, DB], [-1, NS]], channel_multiplier=0))
            pool.sem_inc(ok["ready"], 1)

        @block.sync
        def _(sp):
            sp.wait_ge(ok["zero"], 1)
            sp.dma_start(bias[:, 0:HA], row_bcast(A["b_igate"], P)).then_inc(ok["w_in"], 16)
            sp.dma_start(bias[:, HA:2 * HA], row_bcast(A["b_fgate"], P)).then_inc(ok["w_in"], 16)
            sp.dma_start(gm[:, :], row_bcast(A["g_mlstm"], P)).then_inc(ok["w_in"], 16)
            if sample:
                sp.dma_start(C0[0:HD, :, :, :], A["state_c"].rearrange("b h e d -> e b h d")).then_inc(ok["w_in"], 16)
                sp.dma_start(C0[HD:E1, :, :, :], A["state_n"].rearrange("(a b) h d -> a b h d", a=1)).then_inc(ok["w_in"], 16)
                for q in range(DB):
                    sp.dma_start(mr[q * DT:(q + 1) * DT, :], A["state_m"][q:q + 1, :].broadcast_to([DT, HA])).then_inc(ok["w_in"], 16)

            def load(t, s):
                cols = bass.ds(t * P + row0, R)
                sp.dma_start(X[s][0:R, :], S["nat"][cols, 0:QB]).then_inc(x_in[s], 16)
                sp.dma_start(QT[s][:, :, :], S["qkT"][0:2, :, cols].rearrange("g p t -> p g t")).then_inc(x_in[s], 16)
                for h in range(2):
                    half = slice(h * HD, (h + 1) * HD)
                    sp.dma_start(KZ[s][half, h, :, :], S["qkT"][2:4, half, cols].rearrange("g p t -> p g t")).then_inc(x_in[s], 16)

            def chunk(t, s):
                if not sample:
                    wait_apart(sp, ok["done"], t + 1, passed)
                load(t, s)

            chunks(sp, chunk)

        @block.scalar
        def _(act):
            act.preload_act_table_set("natural_log_exp_and_others")
            act.wait_ge(ok["ready"], 1)

            def chunk(t, s):
                x, n = X[s], t + 1
                r = slice(0, R)

                def run(out, in_, func, after, name, **kw):
                    act.wait_ge(ok[after], n)
                    act.activation(out, in_, func, **kw).then_inc(ok[name], 1)

                act.wait_ge(ok["done"], t + 2)
                run(ex[r, :], nf[r, :], ACT.Exp, "nf", "ex")
                run(sp_[r, :], ex[r, :], ACT.Ln, "ex", "sp", bias=1.0)
                run(OG[r, :], x[r, OA:OA + NA], ACT.Exp, "nf", "og", scale=-1.0)
                run(EX[r, :, :], EX[r, :, :], ACT.Exp, "wx", "wex")
                act.wait_ge(ok["ngs"], n)
                for h in range(HA):
                    ins = act.activation(DD[r, h, :], AM[r, h, :], ACT.Exp, bias=ng[r, h:h + 1])
                ins.then_inc(ok["dec"], 1)
                run(EE[r, :, :], EE[r, :, :], ACT.Exp, "ee", "eex")
                run(ST[r, :, :], pA[r, :, 0:R], ACT.Copy, "st", "stc")
                run(rs[r, :], r1[r, :], ACT.Ln, "ssq", "ln", scale=1.0 / HD, bias=eps[r, :])
                run(rs[r, :], rs[r, :], ACT.Exp, "ln", "rsq", scale=-0.5)
                act.wait_ge(ok["done"], t + 3)
                cols = t * P + row0
                for c in range(2 if sample else 1):
                    act.dma_start(S["yT"][0:2, :, bass.ds(cols + c * NS, R)].rearrange("g p t -> p g t"), YT[:, :, :]).then_inc(y_out, 16)
                act.wait_ge(y_out, (t + 1) * 16 + (16 if sample else 0))
                act.sem_inc(ok["drain"], 1)

            chunks(act, chunk)
            act.wait_ge(ok["tailv"], 1)
            if sample:
                act.dma_start(O["s_c"].rearrange("b h e d -> e b h d"), C1[0:HD, :, :, :]).then_inc(o_out, 16)
                act.dma_start(O["s_n"].rearrange("(a b) h d -> a b h d", a=1), C1[HD:E1, :, :, :]).then_inc(o_out, 16)
                for q in range(DB):
                    act.dma_start(O["s_m"][q:q + 1, :], mr[q * DT:q * DT + 1, :]).then_inc(o_out, 16)
                act.wait_ge(o_out, 16 * (2 + DB))
            else:
                for h in range(HA):
                    d0 = h % 2 * HD
                    act.dma_start(O["p_c"][h], UC[0:HD, h, d0:d0 + HD]).then_inc(o_out, 16)
                    act.dma_start(O["p_n"][h:h + 1, :], UC[HD:E1, h, d0:d0 + HD]).then_inc(o_out, 16)
                act.dma_start(O["p_m"][0:1, :], mr[0:1, :]).then_inc(o_out, 16)
                act.wait_ge(o_out, 16 * (2 * HA + 1))

        @block.vector
        def _(dve):
            for s in range(2):
                for h in range(2):
                    dve.memset(KZ[s][(1 - h) * HD:(2 - h) * HD, h, :, :], 0.0)
            dve.memset(VX[:, :, :], 1.0)
            if not sample:
                dve.memset(mr[:, :], 0.0)
            dve.memset(CT[:, :, :, :], 0.0).then_inc(ok["zero"], 1)
            dve.sem_inc(ok["done"], 2)
            dve.sem_inc(ok["drain"], 1)
            dve.wait_ge(ok["zero"], 1)
            dve.wait_ge(ok["ready"], 1)
            dve.wait_ge(ok["w_in"], 16 * (3 + (2 + DB if sample else 0)))
            if sample:
                for q in range(4):
                    dve.wait_ge(ok["tail"], q + 1)
                    for j in range(4):
                        b, g = (4 * q + j) // 2, j % 2
                        for h in range(2):
                            half = slice(h * HD, (h + 1) * HD)
                            ins = dve.tensor_copy(CT[half, b, 2 * g + h, :], pU[half, j, 0:E1])
                    ins.then_inc(ok["blkm"], 1)

            def chunk(t, s):
                x, n, r = X[s], t + 1, slice(0, R)

                def run(name, ins_of, *after):
                    for a in after:
                        dve.wait_ge(ok[a], n)
                    ins_of().then_inc(ok[name], 1)

                tt = lambda *a: (lambda: dve.tensor_tensor(*a))
                dve.wait_ge(x_in[s], (t - s) * 32 + 64)
                dve.wait_ge(ok["drain"], t + 1)
                run("f", tt(f[r, :], x[r, GF:GF + HA], bias[r, HA:2 * HA], ALU.add))
                run("nf", lambda: dve.scalar_tensor_tensor(out=nf[r, :], in0=f[r, :], scalar=-1.0, in1=f[r, :], op0=ALU.mult, op1=ALU.min), "f")
                dve.tensor_tensor(ig[r, :], x[r, GI:GI + HA], bias[r, 0:HA], ALU.add)
                dve.tensor_copy(VX[r, :, 0:HD], x[r, VA:VA + NA].rearrange("p (h e) -> p h e", e=HD)).then_inc(ok["vx"], 1)
                run("lf", lambda: dve.scalar_tensor_tensor(out=lf[r, :], in0=f[r, :], scalar=0.0, in1=sp_[r, :], op0=ALU.min, op1=ALU.subtract), "sp")
                run("bc", lambda: dve.tensor_copy(bb[r, :], pB[r, 0:HA]), "b", "vx")
                run("a", tt(aa[r, :], ig[r, :], bb[r, :], ALU.subtract), "bc")
                run("da", tt(DA[r, :, :], ident[r, None, 0:R].broadcast_to([R, HA, R]), bc(aa[r, :], R), ALU.mult), "a")
                wait_apart(dve, ok["ab"], n, passed_dve)
                for h in range(HA):
                    ins = dve.tensor_tensor_reduce(out=AM[r, h, :], in0=pA[r, h, 0:R], in1=mask[r, 0:R], scale=1.0, scalar=-3e38,
                                                   op0=ALU.add, op1=ALU.max, accum_out=am[r, h:h + 1])
                ins.then_inc(ok["am"], 1)
                run("g", tt(gg[r, :], am[r, :], mr[r, :], ALU.max), "am")
                run("ngs", lambda: dve.tensor_scalar(ng[r, :], gg[r, :], -1.0, None, ALU.mult), "g")
                dve.tensor_tensor(GM[r, 0:HA], bb[r, :], gg[r, :], ALU.add)
                dve.tensor_copy(GM[r, HA:2 * HA], gg[r, :])
                run("gm", tt(EX[r, 0, :], mr[r, :], gg[r, :], ALU.subtract))
                run("wx", lambda: dve.tensor_scalar(EX[r, 1, :], GM[r, 0:HA], -1.0, None, ALU.mult), "gm")
                run("og1", lambda: dve.tensor_scalar(OG[r, :], OG[r, :], 1.0, None, ALU.add), "og")
                run("og2", lambda: dve.reciprocal(OG[r, :], OG[r, :]), "og1")
                dve.wait_ge(ok["lastr"], n)
                dve.tensor_tensor(EE[r, 0, :], mr[r, :], pB[r, 16 + HA:16 + 2 * HA], ALU.subtract)
                run("ee", tt(EE[r, 1, :], aa[r, :], pB[r, 16 + HA:16 + 2 * HA], ALU.subtract))
                run("sd", lambda: dve.scalar_tensor_tensor(out=SD[r, :, :], in0=pS[r, :, 0:R], scalar=SCALE, in1=DD[r, :, :],
                                                           op0=ALU.mult, op1=ALU.mult), "dec", "s")
                run("kw", lambda: dve.scalar_tensor_tensor(out=KW[r, :, :], in0=x[r, KA:KA + NA].rearrange("p (h e) -> p h e", e=HD),
                                                           scalar=SCALE, in1=bc(EE[r, 1, :], HD), op0=ALU.mult, op1=ALU.mult), "eex")
                if sample:
                    for b in range(DB):
                        dve.tensor_scalar(VM[:, b, :, :], VX[r, :, :], blk[r, b:b + 1], None, ALU.mult)
                        ins = dve.tensor_scalar(DS[:, b, :], EE[r, 0, :], blast[r, b:b + 1], None, ALU.mult)
                    ins.then_inc(ok["vm"], 1)
                run("num", tt(NU[r, :, :], pQ[r, :, :], bc(EX[r, 0, :], E1), ALU.mult), "inter", "wex")
                run("num2", tt(NU[r, :, :], NU[r, :, :], pI[r, :, :], ALU.add), "intra", "num")
                den = NU[r, :, HD:E1].rearrange("p h a -> p (h a)")
                run("den", lambda: dve.scalar_tensor_tensor(out=dn[r, :], in0=den, scalar=-1.0, in1=den, op0=ALU.mult, op1=ALU.max), "num2")
                run("den2", tt(dn[r, :], dn[r, :], EX[r, 1, :], ALU.max), "den")
                run("rden", lambda: dve.reciprocal(dn[r, :], dn[r, :]), "den2")
                run("h", tt(HH[r, :, :], NU[r, :, 0:HD], bc(dn[r, :], HD), ALU.mult), "rden")
                run("hsq", tt(HS[r, :, :], HH[r, :, :], HH[r, :, :], ALU.mult), "h")
                run("ssq", lambda: dve.reduce_sum(r1[r, :], HS[r, :, :], AX.X), "hsq")
                run("y1", tt(OG[r, :], OG[r, :], gm[r, :], ALU.mult), "og2")
                run("y2", tt(YY[r, :, :], HH[r, :, :], OG[r, :].rearrange("p (h e) -> p h e", e=HD), ALU.mult), "y1")
                run("y3", tt(YY[r, :, :], YY[r, :, :], bc(rs[r, :], HD), ALU.mult), "rsq", "y2")
                if not sample:
                    dve.wait_ge(ok["up"], n)
                    for h in range(HA):
                        half = slice(h % 2 * HD, (h % 2 + 1) * HD)
                        dve.scalar_tensor_tensor(out=CT[half, 0, h, :], in0=CT[half, 0, h, :], scalar=EE[half, 0, h:h + 1],
                                                 in1=pU[half, h, 0:E1], op0=ALU.mult, op1=ALU.add)
                dve.tensor_copy(mr[r, :], pB[r, 16:16 + HA]).then_inc(ok["ct"], 1)
                dve.wait_ge(ok["ct"], n)
                dve.wait_ge(ok["yt"], n)
                dve.tensor_copy(YT[:, :, :], pS[:, 0:2, 0:R]).then_inc(ok["done"], 1)

            if sample:
                dve.wait_ge(x_in[0], 64)
                for g in range(2):
                    ins = dve.tensor_tensor(QM[:, g, :, :], QT[0][:, g, None, :].broadcast_to([P, DB, NS]), bcol[:, :, :], ALU.mult)
                ins.then_inc(ok["blkm"], 1)
            chunks(dve, chunk)
            if sample:
                dve.wait_ge(ok["vm"], 1)
                dve.wait_ge(ok["up"], 1)
                for half in range(4):
                    dve.wait_ge(ok["tail"], 4 + half + 1)
                    sl = slice(2 * half, 2 * half + 2)
                    dec = pB[0:E1, 64 + half * 2 * HA:64 + (half + 1) * 2 * HA].rearrange("p (b h) -> p b h", b=2)
                    for b in range(2):
                        ins = dve.tensor_tensor(C1[:, 2 * half + b, :, :], C0[:, 2 * half + b, :, :],
                                                dec[:, b, :, None].broadcast_to([E1, HA, HD]), ALU.mult)
                    ins.then_inc(ok["y1"], 1)
                    dve.wait_ge(ok["y1"], 1 + half + 1)
                    dve.tensor_tensor(C1[:, sl, :, :].rearrange("p b h d -> p (b h d)"), C1[:, sl, :, :].rearrange("p b h d -> p (b h d)"),
                                      pC[0:E1, half % 2, :], ALU.add).then_inc(ok["num"], 1)
                dve.wait_ge(ok["num"], 5)
            else:
                dve.wait_ge(ok["tail"], 1)
                dve.tensor_copy(UC[0:E1, :, :], pU[0:E1, :, :]).then_inc(ok["num"], 1)
                dve.wait_ge(ok["num"], NT + 1)
            dve.sem_inc(ok["tailv"], 1)

        @block.tensor
        def _(pe):
            pe.wait_ge(ok["ready"], 1)
            pe.wait_ge(ok["zero"], 1)
            if sample:
                pe.wait_ge(ok["w_in"], 16 * (5 + DB))
                for q in range(4):
                    if q:
                        pe.wait_ge(ok["blkm"], q)
                    for j in range(4):
                        b, g = (4 * q + j) // 2, j % 2
                        ins = pe.transpose(pU[:, j, 0:E1], C0[:, b, 2 * g:2 * g + 2, :].rearrange("p h d -> p (h d)"), ident[0:E1, 0:E1])
                    ins.then_inc(ok["tail"], 1)
                pe.wait_ge(ok["blkm"], 5)

            def chunk(t, s):
                n, r = t + 1, slice(0, R)
                pe.wait_ge(ok["done"], t + 2)
                pe.wait_ge(x_in[s], (t - s) * 32 + 64)
                for h in range(HA):
                    ins = pe.matmul(pS[r, h, 0:R], QT[s][:, h // 2, :], KZ[s][:, h % 2, h // 2, :], start=True, stop=True)
                ins.then_inc(ok["s"], 1)
                if sample:
                    for h in range(HA):
                        for b in range(DB):
                            ins = pe.matmul(pQ[r, h, :], QM[:, h // 2, b, :], CT[:, b, h, :], start=(b == 0), stop=(b == DB - 1))
                else:
                    for h in range(HA):
                        ins = pe.matmul(pQ[r, h, :], QT[s][:, h // 2, :], CT[:, 0, h, :], start=True, stop=True)
                ins.then_inc(ok["inter"], 1)
                pe.wait_ge(ok["lf"], n)
                pe.matmul(pB[r, 0:HA], tri[r, 0:R], lf[r, :], start=True, stop=True).then_inc(ok["b"], 1)
                pe.wait_ge(ok["da"], n)
                pe.matmul(pA[r, :, 0:R], ones[r, 0:R], DA[r, :, :], start=True, stop=True).then_inc(ok["ab"], 1)
                pe.wait_ge(ok["gm"], n)
                pe.matmul(pB[r, 16:16 + 2 * HA], last[r, 0:R], GM[r, :], start=True, stop=True).then_inc(ok["lastr"], 1)
                pe.wait_ge(ok["sd"], n)
                for h in range(HA):
                    ins = pe.transpose(pA[r, h, 0:R], SD[r, h, :], ident[r, 0:R])
                ins.then_inc(ok["st"], 1)
                pe.wait_ge(ok["kw"], n)
                if sample:
                    pe.wait_ge(ok["vm"], 1)
                    pe.matmul(pB[0:E1, 64:64 + DB * HA], ones[r, 0:E1], DS[:, :, :].rearrange("p b h -> p (b h)"), start=True, stop=True).then_inc(ok["up"], 1)
                else:
                    for h in range(HA):
                        ins = pe.matmul(pU[:, h, 0:E1], KW[:, h // 2 * 2:h // 2 * 2 + 2, :].rearrange("p h d -> p (h d)"), VX[:, h, :], start=True, stop=True)
                    ins.then_inc(ok["up"], 1)
                pe.wait_ge(ok["stc"], n)
                for h in range(HA):
                    ins = pe.matmul(pI[r, h, :], ST[r, h, :], VX[r, h, :], start=True, stop=True)
                ins.then_inc(ok["intra"], 1)
                pe.wait_ge(ok["y3"], n)
                for g in range(2):
                    ins = pe.transpose(pS[:, g, 0:R], YY[r, 2 * g:2 * g + 2, :].rearrange("p h e -> p (h e)"), ident[r, 0:R])
                ins.then_inc(ok["yt"], 1)

            chunks(pe, chunk)
            if sample:
                for half in range(4):
                    if half > 1:
                        pe.wait_ge(ok["num"], half)
                    for j in range(2):
                        for h in range(HA):
                            b = 2 * half + j
                            ins = pe.matmul(pC[0:E1, half % 2, (j * HA + h) * HD:(j * HA + h + 1) * HD], VM[:, b, h, :], KW[0:NS, h, :],
                                            start=True, stop=True)
                    ins.then_inc(ok["tail"], 1)
            else:
                pe.wait_ge(ok["done"], NT + 2)
                for h in range(HA):
                    ins = pe.transpose(pU[0:E1, h, :], CT[:, 0, h, :], ident[:, :])
                ins.then_inc(ok["tail"], 1)


def mlstm_phase(nc, A, S, O):
    mlstm_chunks(nc, A, S, O, False)
    mlstm_chunks(nc, A, S, O, True)


def window_masks():
    import math
    lg = [NEG, 0.0, math.log(2.0), math.log(3.0)]

    def count(d):
        return sum(0 <= d <= w and d % dil == 0 for w, dil in ((128, 1), (512, 4), (2048, 16)))

    cached = [[[lg[count(WIN + t - pos)] for t in range(DT)] for pos in
               [256 * j + 16 * (p // 8) + p % 8 if j < 6 else 1536 + 128 * (j - 6) + p for j in range(10)]] for p in range(P)]
    new = [[[lg[count(t - p % DT)] if b == p // DT else NEG for t in range(DT)] for b in range(DB)] for p in range(P)]
    return cached, new


def dilated_sample_phase(nc, A, S, O):
    PAIRS, HT_, TL = 3, 2 * DT, 10
    C = PAIRS * HT_
    with ExitStack() as ctx:
        m = Mem(nc, ctx, "sd")
        K = [m.sb(f"K{i}", [P, TL, NB]) for i in range(2)]
        V = [m.sb(f"V{i}", [P, TL, NB]) for i in range(2)]
        KT = m.sb("KT", [P, 32, P])
        QL = m.sb("QL", [P, PAIRS, NS])
        KN = m.sb("KN", [P, PAIRS, NS])
        VN = m.sb("VN", [P, NB])
        QD = m.sb("QD", [P, DB, PAIRS, HT_])
        MW = m.sb("MW", [P, TL, DT])
        MN = m.sb("MN", [P, DB, DT])
        SN = m.sb("SN", [P, DB, C])
        Z = m.sb("Z", [P, TL + 1, C])
        mx = m.sb("mx", [P, C])
        mc = m.sb("mc", [C, 1])
        md = m.sb("md", [C, C])
        sm = m.sb("sm", [P, C])
        rd = m.sb("rd", [P, C])
        YA = m.sb("YA", [P, PAIRS, NS])
        ident = m.sb("ident", [P, P])
        ones = m.sb("ones", [P, P])
        KTP = [m.ps(f"KTP{i}", [P, 4, P]) for i in range(4)]
        ZP = m.ps("ZP", [P, TL, C])
        SP = m.ps("SP", [P, 512])
        YP = m.ps("YP", [P, PAIRS, HT_])
        names = ["consts", "new_in", "qd", "zn", "sn", "qdz", "kt_ps", "kt_a", "kt_v", "z", "zm", "zn2", "mx", "mt", "mc", "md", "mb",
                 "sub", "e", "sum", "den", "rd", "av", "y"]
        ok = {x: m.sem(x + "_ok") for x in names}
        passed, passed_pe = m.sem("passed"), m.sem("passed_pe")
        kv_in = [m.sem(f"kv_in{i}") for i in range(2)]
        y_out = m.sem("y_out")
        block = ctx.enter_context(nc.Block())

        def seqs(eng, step, first=0, last=DB):
            with eng.Fori(first // 2, last // 2) as i:
                for s in range(2):
                    step(i * 2 + s, s)

        @block.gpsimd
        def _(pool):
            pool.memset(ident[:, :], 0.0)
            pool.memset(ones[:, :], 1.0).then_inc(ok["consts"], 1)
            pool.wait_ge(ok["consts"], 1)
            pool.affine_select(out=ident[:, :], in_=ident[:, :], compare_op=ALU.not_equal, fill=1.0, base=0,
                               pattern=[[-1, P]], channel_multiplier=1).then_inc(ok["consts"], 1)

        @block.sync
        def _(sp):
            for g, x in ((GB, QL), (GB + 3, KN)):
                sp.dma_start(x[:, :, :], S["qkT"][g:g + 3, :, SEQ:SEQ + NS].rearrange("g p t -> p g t")).then_inc(ok["new_in"], 16)
            sp.dma_start(VN[:, :], S["nat"][SEQ:TP, VB:QC]).then_inc(ok["new_in"], 16)
            sp.dma_start(MW[:, :, :], A["window_mask"][:, 0:TL, :]).then_inc(ok["new_in"], 16)
            sp.dma_start(MN[:, :, :], A["window_mask"][:, TL:TL + DB, :]).then_inc(ok["new_in"], 16)

            def step(b, s):
                wait_apart(sp, ok["av"], b + 1, passed)
                for dst, src in ((K, A["cache_win_k"]), (V, A["cache_win_v"])):
                    seq = src[bass.ds(b, 1), :, :].rearrange("a w c -> (a w) c")
                    far = seq[0:1536, :].rearrange("(j n r) c -> j n r c", j=6, r=16)
                    for j in range(6):
                        sp.dma_start(dst[s][:, j, :], far[j, :, 0:8, :]).then_inc(kv_in[s], 16)
                    sp.dma_start(dst[s][:, 6:TL, :], seq[1536:WIN, :].rearrange("(j p) c -> p j c", p=P)).then_inc(kv_in[s], 16)

            seqs(sp, step)

        @block.scalar
        def _(act):
            act.preload_act_table_set("natural_log_exp_and_others")

            def turned(b):
                for j in (0, 2, 4, 6):
                    act.wait_ge(ok["kt_ps"], b * 8 + j + 1)
                    act.activation(KT[:, 4 * j:4 * j + 4, :], KTP[j % 4][:, :, :], ACT.Copy).then_inc(ok["kt_a"], 1)

            def step(b, s, more=True):
                if more:
                    turned(b + 1)
                act.wait_ge(ok["sub"], b + 1)
                act.activation(Z[:, :, :], Z[:, :, :], ACT.Exp).then_inc(ok["e"], 1)

            turned(0)
            seqs(act, step, 0, DB - 2)
            step(DB - 2, 0)
            step(DB - 1, 1, False)
            act.wait_ge(ok["y"], DB + 1)
            for c in range(2):
                act.dma_start(S["yT"][2:5, :, SEQ + c * NS:SEQ + (c + 1) * NS].rearrange("g p t -> p g t"), YA[:, :, :]).then_inc(y_out, 16)
            act.wait_ge(y_out, 32)

        @block.vector
        def _(dve):
            dve.memset(SN[NS:P, :, :], NEG)
            dve.memset(QD[:, :, :, :], 0.0).then_inc(ok["qdz"], 1)
            dve.wait_ge(ok["qdz"], 1)
            dve.wait_ge(ok["new_in"], 80)
            for h in range(2):
                half = slice(h * HD, (h + 1) * HD)
                ins = dve.tensor_scalar(QD[half, :, :, h * DT:(h + 1) * DT].rearrange("p b g t -> p g b t"),
                                        QL[half, :, :].rearrange("p g (b t) -> p g b t", t=DT), SCALE, None, ALU.mult)
            ins.then_inc(ok["qd"], 1)
            dve.wait_ge(ok["zn"], 1)
            for g in range(PAIRS):
                for h in range(2):
                    a = g * HT_ + h * DT
                    ins = dve.tensor_tensor(SN[0:NS, :, a:a + DT], KTP[0][0:NS, g, :].rearrange("p (b c) -> p b c", c=HT_)[:, :, h * DT:(h + 1) * DT],
                                            MN[0:NS, :, :], ALU.add)
            ins.then_inc(ok["sn"], 1)
            dve.wait_ge(ok["sn"], 1)
            dve.sem_inc(ok["kt_v"], 2)
            dve.sem_inc(ok["kt_a"], 2)
            dve.sem_inc(ok["y"], 1)

            def turned(b):
                for j in (1, 3, 5, 7):
                    dve.wait_ge(ok["kt_ps"], b * 8 + j + 1)
                    n = 4 if j < 7 else 2
                    dve.tensor_copy(KT[:, 4 * j:4 * j + n, :], KTP[j % 4][:, 0:n, :]).then_inc(ok["kt_v"], 1)

            def step(b, s, more=True):
                dve.wait_ge(ok["av"], b + 2)
                dve.tensor_copy(Z[:, TL, :], SN[:, bass.ds(b, 1), :].rearrange("p a c -> p (a c)"))
                dve.wait_ge(ok["z"], b + 1)
                dve.tensor_tensor(Z[:, 0:TL, :].rearrange("p j (h t) -> p j h t", t=DT), ZP[:, :, :].rearrange("p j (h t) -> p j h t", t=DT),
                                  MW[:, :, None, :].broadcast_to([P, TL, 2 * PAIRS, DT]), ALU.add).then_inc(ok["zm"], 1)
                dve.wait_ge(ok["zm"], b + 1)
                dve.tensor_reduce(mx[:, :], Z[:, :, :].rearrange("p j c -> p c j"), AX.X, ALU.max).then_inc(ok["mx"], 1)
                if more:
                    turned(b + 1)
                dve.wait_ge(ok["mt"], b + 1)
                dve.tensor_reduce(mc[:, :], SP[0:C, 0:P], AX.X, ALU.max).then_inc(ok["mc"], 1)
                dve.wait_ge(ok["mc"], b + 1)
                dve.tensor_scalar(md[:, :], ident[0:C, 0:C], mc[:, :], None, ALU.mult).then_inc(ok["md"], 1)
                dve.wait_ge(ok["mb"], b + 1)
                dve.tensor_tensor(Z[:, :, :], Z[:, :, :], SP[:, None, P:P + C].broadcast_to([P, TL + 1, C]), ALU.subtract).then_inc(ok["sub"], 1)
                dve.wait_ge(ok["e"], b + 1)
                dve.tensor_reduce(sm[:, :], Z[:, :, :].rearrange("p j c -> p c j"), AX.X, ALU.add).then_inc(ok["sum"], 1)
                dve.wait_ge(ok["den"], b + 1)
                dve.reciprocal(rd[:, :], SP[:, 2 * P:2 * P + C]).then_inc(ok["rd"], 1)
                dve.wait_ge(ok["rd"], b + 1)
                dve.wait_ge(ok["av"], b + 3)
                for h in range(2):
                    half = slice(h * HD, (h + 1) * HD)
                    rv = rd[half, :].rearrange("p (g x t) -> p g x t", g=PAIRS, x=2)[:, :, h, :]
                    ins = dve.tensor_tensor(YA[half, :, bass.ds(b * DT, DT)], YP[half, :, h * DT:(h + 1) * DT], rv, ALU.mult)
                ins.then_inc(ok["y"], 1)

            turned(0)
            seqs(dve, step, 0, DB - 2)
            step(DB - 2, 0)
            step(DB - 1, 1, False)

        @block.tensor
        def _(pe):
            pe.wait_ge(ok["consts"], 2)
            pe.wait_ge(ok["qd"], 1)
            for g in range(PAIRS):
                ins = pe.matmul(KTP[0][0:NS, g, :], KN[:, g, :], QD[:, :, g, :], start=True, stop=True)
            ins.then_inc(ok["zn"], 1)
            pe.wait_ge(ok["sn"], 1)
            pe.sem_inc(ok["av"], 2)

            def turn(b, s):
                pe.wait_ge(kv_in[s], (b - s) * 112 + 224)
                for j in range(8):
                    pe.wait_ge(ok["kt_a" if j % 2 == 0 else "kt_v"], b * 4 + j // 2 + 1)
                    for i in range(4 if j < 7 else 2):
                        x = 4 * j + i
                        ins = pe.transpose(KTP[j % 4][:, i, :], K[s][:, x // PAIRS, x % PAIRS * P:(x % PAIRS + 1) * P], ident[:, :])
                    ins.then_inc(ok["kt_ps"], 1)

            def rest(b, s, more):
                pe.wait_ge(ok["kt_a"], b * 4 + 6)
                pe.wait_ge(ok["kt_v"], b * 4 + 6)
                for j in range(TL):
                    for g in range(PAIRS):
                        ins = pe.matmul(ZP[:, j, g * HT_:(g + 1) * HT_], KT[:, j * PAIRS + g, :],
                                        QD[:, bass.ds(b, 1), g, :].rearrange("p a c -> p (a c)"), start=True, stop=True)
                ins.then_inc(ok["z"], 1)
                if more:
                    turn(b + 1, 1 - s)
                wait_apart(pe, ok["mx"], b + 1, passed_pe)
                pe.transpose(SP[0:C, 0:P], mx[:, :], ident[:, :]).then_inc(ok["mt"], 1)
                pe.wait_ge(ok["md"], b + 1)
                pe.matmul(SP[:, P:P + C], ones[0:C, :], md[:, :], start=True, stop=True).then_inc(ok["mb"], 1)
                pe.wait_ge(ok["sum"], b + 1)
                pe.matmul(SP[:, 2 * P:2 * P + C], ones[:, :], sm[:, :], start=True, stop=True).then_inc(ok["den"], 1)
                pe.wait_ge(ok["y"], b + 1)
                for j in range(TL + 1):
                    for g in range(PAIRS):
                        cols, rows = slice(g * P, (g + 1) * P), P
                        ins = pe.matmul(YP[:, g, :], V[s][:, j, cols] if j < TL else VN[:, cols], Z[:, j, g * HT_:(g + 1) * HT_],
                                        start=(j == 0 and g == 0), stop=True, skip_group_check=True)
                ins.then_inc(ok["av"], 1)

            turn(0, 0)
            seqs(pe, lambda b, s: rest(b, s, True), 0, DB - 2)
            rest(DB - 2, 0, True)
            rest(DB - 1, 1, False)


def stick_sample_phase(nc, A, S, O):
    NP, PAIRS, HT_ = 8, 3, 2 * DT
    NG, C = PAGES // NP, PAIRS * HT_
    with ExitStack() as ctx:
        m = Mem(nc, ctx, "sc")
        table = m.sb("table", [1, DB * PAGES], I32)
        KP = [m.sb(f"KP{i}", [P, NP, NC]) for i in range(2)]
        VP = [m.sb(f"VP{i}", [P, NP, NC]) for i in range(2)]
        KT = [m.sb(f"KT{i}", [P, NP * PAIRS, P]) for i in range(2)]
        QL = m.sb("QL", [P, PAIRS, NS])
        KN = m.sb("KN", [P, PAIRS, NS])
        VN = m.sb("VN", [NS, NC])
        QD = m.sb("QD", [P, DB, PAIRS, HT_])
        bsb = m.sb("bsb", [P, HC])
        BB = m.sb("BB", [P, NP, C])
        ZB = [m.sb(f"ZB{i}", [P, NP, C]) for i in range(2)]
        E = m.sb("E", [P, NP, C])
        L = [m.sb(f"L{i}", [P, NP, C]) for i in range(2)]
        SL = [m.sb(f"SL{i}", [P, NP + 1, C]) for i in range(2)]
        AR = m.sb("AR", [P, NP, C])
        T = [m.sb(f"T{i}", [P, NP, C]) for i in range(2)]
        SI = m.sb("SI", [P, DB, C])
        YN = m.sb("YN", [P, DB, PAIRS, HT_])
        YA = m.sb("YA", [P, PAIRS, NS])
        maskn = m.sb("maskn", [NS, DB, HT_])
        ident = m.sb("ident", [P, P])
        ntri = m.sb("ntri", [P, P])
        nones = m.sb("nones", [P, P])
        KTP = [m.ps(f"KTP{i}", [P, 4, P]) for i in range(4)]
        ZP = m.ps("ZP", [P, NP, C])
        AP_ = m.ps("AP", [P, NP, C])
        YP = [m.ps(f"YP{i}", [P, PAIRS, HT_]) for i in range(2)]
        consts = m.sem("consts")
        t_in = m.sem("t_in")
        passed = m.sem("passed")
        new_in = m.sem("new_in")
        k_in = [m.sem(f"k_in{i}") for i in range(2)]
        v_in = [m.sem(f"v_in{i}") for i in range(2)]
        setup = m.sem("setup")
        setup_v = m.sem("setup_v")
        setup_e = m.sem("setup_e")
        setup_p = m.sem("setup_p")
        kt_ps = m.sem("kt_ps")
        kt_a = m.sem("kt_a")
        kt_v = m.sem("kt_v")
        z_ok = m.sem("z_ok")
        zb_ok = m.sem("zb_ok")
        zc_ok = m.sem("zc_ok")
        e_ok = m.sem("e_ok")
        sp_ok = m.sem("sp_ok")
        l_ok = m.sem("l_ok")
        s_ok = m.sem("s_ok")
        arg_ok = m.sem("arg_ok")
        ar_ok = m.sem("ar_ok")
        a_ok = m.sem("a_ok")
        av_ok = m.sem("av_ok")
        yc_ok = m.sem("yc_ok")
        y_out = m.sem("y_out")
        block = ctx.enter_context(nc.Block())
        qs, ks = S["qkT"][GC:GC + 3, :, SEQ:SEQ + NS], S["qkT"][GC + 3:GC + 6, :, SEQ:SEQ + NS]

        def sequences(group):
            def run(eng):
                group(0, 0, 0, (0, 1))
                with eng.Fori(1, DB) as b:
                    for q in range(1, NG):
                        group(b - 1, q, (b - 1) * NG + q, (b - 1, q + 1) if q + 1 < NG else (b, 0))
                    group(b, 0, b * NG, (b, 1))
                for q in range(1, NG):
                    group(DB - 1, q, (DB - 1) * NG + q, (DB - 1, q + 1) if q + 1 < NG else None)
            return run

        @block.gpsimd
        def _(pool):
            pool.memset(ident[:, :], 0.0)
            pool.memset(maskn[:, :, :], 0.0)
            for t in (ntri, nones):
                ins = pool.memset(t[:, :], -1.0)
            ins.then_inc(consts, 1)
            pool.wait_ge(consts, 1)
            pool.affine_select(out=ident[:, :], in_=ident[:, :], compare_op=ALU.not_equal, fill=1.0, base=0,
                               pattern=[[-1, P]], channel_multiplier=1).then_inc(consts, 1)
            pool.affine_select(out=ntri[:, :], in_=ntri[:, :], compare_op=ALU.is_ge, fill=0.0, base=0,
                               pattern=[[-1, P]], channel_multiplier=1).then_inc(consts, 1)
            pool.wait_ge(consts, 3)
            new = maskn[:, :, :].rearrange("p b (h t) -> p b h t", h=2)
            pool.affine_select(out=new, in_=new, compare_op=ALU.is_ge, fill=NEG, base=0,
                               pattern=[[-DT, DB], [0, 2], [0, DT]], channel_multiplier=1).then_inc(consts, 1)
            pool.wait_ge(consts, 4)
            pool.affine_select(out=new, in_=new, compare_op=ALU.is_gt, fill=NEG, base=0,
                               pattern=[[DT, DB], [0, 2], [1, DT]], channel_multiplier=-1).then_inc(consts, 1)

        @block.sync
        def _(sp):
            sp.dma_start(table[:, :], A["page_table"].rearrange("(a b) j -> a (b j)", a=1)).then_inc(t_in, 16)
            sp.dma_start(QL[:, :, :], qs.rearrange("g p t -> p g t")).then_inc(new_in, 16)
            sp.dma_start(KN[:, :, :], ks.rearrange("g p t -> p g t")).then_inc(new_in, 16)
            sp.dma_start(VN[:, :], O["s_sv"]).then_inc(new_in, 16)
            sp.dma_start(bsb[:, :], row_bcast(A["b_sb"], P)).then_inc(new_in, 16)
            sp.wait_ge(t_in, 16)

            def load(dst, src, landed, b, q):
                s = q % 2
                _, pages = nc.values_load_multi_w_load_instructions(
                    table[0:1, bass.ds(b * PAGES + (PAGES - (q + 1) * NP), NP)], engines=[mybir.EngineType.SP], min_val=0,
                    max_val=A["cache_sb_k"].shape[0] - 1)
                for r in range(NP):
                    sp.dma_start(dst[s][:, r, :], src[bass.ds(pages[NP - 1 - r], 1), :, :].rearrange("a p c -> p (a c)")).then_inc(landed[s], 16)

            def group(b, q, n, nxt):
                if nxt:
                    if not (isinstance(n, int) and n == 0):
                        wait_apart(sp, kt_ps, n * 6, passed)
                    load(KP, A["cache_sb_k"], k_in, *nxt)
                wait_apart(sp, av_ok, n + 1, passed)
                load(VP, A["cache_sb_v"], v_in, b, q)

            load(KP, A["cache_sb_k"], k_in, 0, 0)
            sequences(group)(sp)

        @block.scalar
        def _(act):
            act.preload_act_table_set("natural_log_exp_and_others")
            act.wait_ge(setup, 5)
            en = E[0:NS, :, :]
            act.activation(en, en, ACT.Exp).then_inc(setup_e, 1)
            act.wait_ge(setup_e, 1)
            act.activation(en, en, ACT.Ln, bias=1.0).then_inc(setup_e, 1)
            act.wait_ge(setup, 7)
            act.activation(T[0][0:NS, :, :], AR[0:NS, :, :], ACT.Exp).then_inc(setup_e, 1)

            def weights(n, s):
                act.wait_ge(ar_ok, n + 2)
                act.activation(T[s][:, :, :], AR[:, :, :], ACT.Exp).then_inc(a_ok, 1)

            def copies(n, q):
                for j in (0, 2, 4):
                    act.wait_ge(kt_ps, n * 6 + j + 1)
                    act.activation(KT[q % 2][:, 4 * j:4 * j + 4, :], KTP[(6 * q + j) % 4][:, :, :], ACT.Copy).then_inc(kt_a, 1)

            def group(b, q, n, nxt):
                act.wait_ge(zc_ok, n + 1)
                act.activation(E[:, :, :], E[:, :, :], ACT.Exp).then_inc(e_ok, 1)
                act.wait_ge(e_ok, n + 1)
                act.activation(E[:, :, :], E[:, :, :], ACT.Ln, bias=1.0).then_inc(sp_ok, 1)
                if not (isinstance(n, int) and n == 0):
                    weights(n - 1, 1 - q % 2)
                if nxt:
                    copies(n + 1, nxt[1])

            copies(0, 0)
            sequences(group)(act)
            weights(DB * NG - 1, 1)
            for half in range(2):
                act.wait_ge(yc_ok, DB + 2)
                act.dma_start(S["yT"][5:8, :, SEQ + half * NS:SEQ + (half + 1) * NS].rearrange("g p t -> p g t"), YA[:, :, :]).then_inc(y_out, 16)
            act.wait_ge(y_out, 32)

        @block.vector
        def _(dve):
            dve.wait_ge(new_in, 64)
            count = [0]

            def then(ins):
                count[0] += 1
                ins.then_inc(setup, 1)
                dve.wait_ge(setup, count[0])

            dve.memset(SI[:, :, :], 0.0)
            dve.tensor_copy(BB[:, 0, :].rearrange("p (h t) -> p h t", t=DT), bsb[:, :, None].broadcast_to([P, HC, DT]))
            then(dve.memset(QD[:, :, :, :], 0.0))
            for h in range(2):
                half = slice(h * HD, (h + 1) * HD)
                ins = dve.tensor_scalar(QD[half, :, :, h * DT:(h + 1) * DT].rearrange("p b g t -> p g b t"),
                                        QL[half, :, :].rearrange("p g (b t) -> p g b t", t=DT), SCALE, None, ALU.mult)
            then(ins)
            then(dve.tensor_copy(BB[:, 1:NP, :], BB[:, 0:1, :].broadcast_to([P, NP - 1, C])))
            dve.wait_ge(setup_p, 1)
            dve.wait_ge(consts, 5)
            zn, zb = ZP[0:NS, :, :], ZB[0][0:NS, :, :]
            then(dve.tensor_tensor(zb, zn, BB[0:NS, :, :], ALU.add))
            for g in range(PAIRS):
                ins = dve.tensor_tensor(ZB[1][0:NS, :, g * HT_:(g + 1) * HT_], ZB[0][0:NS, :, g * HT_:(g + 1) * HT_], maskn[:, :, :], ALU.add)
            ins.then_inc(setup_v, 1)
            dve.wait_ge(setup_v, 1)
            then(dve.tensor_scalar(E[0:NS, :, :], ZB[1][0:NS, :, :], 40.0, None, ALU.min))
            dve.wait_ge(setup_e, 2)
            then(dve.tensor_tensor(SI[0:NS, :, :], ZB[1][0:NS, :, :], E[0:NS, :, :], ALU.max))
            dve.wait_ge(setup_p, 2)
            then(dve.tensor_tensor(AR[0:NS, :, :], ZB[1][0:NS, :, :], AP_[0:NS, :, :], ALU.add))
            dve.wait_ge(setup_p, 3)
            for g in range(PAIRS):
                ins = dve.tensor_copy(YN[:, :, g, :], KTP[0][:, g, :].rearrange("p (b c) -> p b c", c=HT_))
            then(ins)
            dve.sem_inc(kt_v, 2)
            dve.sem_inc(kt_a, 2)
            dve.sem_inc(yc_ok, 2)

            def exponents(n, s):
                dve.wait_ge(arg_ok, n + 1)
                dve.wait_ge(a_ok, n + 1)
                dve.tensor_tensor(AR[:, :, :], ZB[s][:, :, :], AP_[:, :, :], ALU.add).then_inc(ar_ok, 1)

            def output(b, q_next):
                dve.wait_ge(av_ok, (b + 1) * NG + 2)
                for h in range(2):
                    half = slice(h * HD, (h + 1) * HD)
                    src = YP[0][half, :, h * DT:(h + 1) * DT]
                    yn = YN[half, bass.ds(b, 1), :, h * DT:(h + 1) * DT].rearrange("p a g t -> p (a g) t")
                    ins = dve.tensor_tensor(YA[half, :, bass.ds(b * DT, DT)], src, yn, ALU.add)
                ins.then_inc(yc_ok, 1)

            def copy(n, q, j):
                dve.wait_ge(kt_ps, n * 6 + j + 1)
                dve.tensor_copy(KT[q % 2][:, 4 * j:4 * j + 4, :], KTP[(6 * q + j) % 4][:, :, :]).then_inc(kt_v, 1)

            def group(b, q, n, nxt):
                s = q % 2
                first = isinstance(n, int) and n == 0
                dve.wait_ge(z_ok, n + 3)
                dve.tensor_tensor(ZB[s][:, :, :], ZP[:, :, :], BB[:, :, :], ALU.add).then_inc(zb_ok, 1)
                dve.wait_ge(zb_ok, n + 2)
                dve.wait_ge(l_ok, n + 1)
                dve.tensor_scalar(E[:, :, :], ZB[s][:, :, :], 40.0, None, ALU.min).then_inc(zc_ok, 1)
                if not first:
                    exponents(n - 1, 1 - s)
                if q == 0:
                    src = SI[:, bass.ds(b, 1), :].rearrange("p a c -> p (a c)")
                else:
                    src = SL[1 - s][:, NP, :]
                dve.tensor_copy(SL[s][:, 0, :], src).then_inc(s_ok, 1)
                if nxt:
                    copy(n + 1, nxt[1], 1)
                dve.wait_ge(sp_ok, n + 1)
                dve.tensor_tensor(L[s][:, :, :], ZB[s][:, :, :], E[:, :, :], ALU.max).then_inc(l_ok, 1)
                dve.wait_ge(l_ok, n + 2)
                for r in range(NP):
                    dve.wait_ge(s_ok, n * (NP + 1) + r + 1)
                    dve.tensor_tensor(SL[s][:, r + 1, :], SL[s][:, r, :], L[s][:, r, :], ALU.add).then_inc(s_ok, 1)
                    if nxt and r in (3, 5):
                        copy(n + 1, nxt[1], r if r == 5 else 3)
                dve.wait_ge(s_ok, n * (NP + 1) + NP + 1)
                if q == 0 and not first:
                    output(b - 1, q)

            dve.sem_inc(l_ok, 1)
            dve.sem_inc(zb_ok, 1)
            dve.sem_inc(ar_ok, 1)
            dve.sem_inc(a_ok, 1)
            copy(0, 0, 1)
            copy(0, 0, 3)
            copy(0, 0, 5)
            sequences(group)(dve)
            exponents(DB * NG - 1, 1)
            output(DB - 1, 0)

        @block.tensor
        def _(pe):
            pe.wait_ge(consts, 5)
            pe.wait_ge(setup, 2)
            for g in range(PAIRS):
                ins = pe.matmul(ZP[0:NS, :, g * HT_:(g + 1) * HT_], KN[:, g, :], QD[:, :, g, :], start=True, stop=True)
            ins.then_inc(setup_p, 1)
            pe.wait_ge(setup, 6)
            pe.matmul(AP_[0:NS, :, :], ntri[0:NS, 0:NS], SI[0:NS, :, :], start=True, stop=True).then_inc(setup_p, 1)
            pe.wait_ge(setup_e, 3)
            for g in range(PAIRS):
                ins = pe.matmul(KTP[0][:, g, :], VN[:, g * P:(g + 1) * P], T[0][0:NS, :, g * HT_:(g + 1) * HT_], start=True, stop=True)
            ins.then_inc(setup_p, 1)
            pe.wait_ge(setup, 8)
            pe.sem_inc(z_ok, 2)
            pe.sem_inc(av_ok, 2)

            def cumulate(n, s):
                pe.wait_ge(s_ok, (n + 1) * (NP + 1))
                pe.wait_ge(ar_ok, n + 1)
                pe.matmul(AP_[:, :, :], ntri[:, :], L[s][:, :, :], start=True, stop=False)
                pe.matmul(AP_[:, :, :], nones[:, :], SL[s][:, 0:NP, :], start=False, stop=True).then_inc(arg_ok, 1)

            def values(n, q, b):
                s = q % 2
                pe.wait_ge(v_in[s], (b * (NG // 2) + q // 2) * (16 * NP) + 16 * NP)
                pe.wait_ge(a_ok, n + 2)
                if q == 0:
                    pe.wait_ge(yc_ok, b + 2)
                for r in range(NP):
                    for g in range(PAIRS):
                        ins = pe.matmul(YP[0][:, g, :], VP[s][:, r, g * P:(g + 1) * P], T[s][:, r, g * HT_:(g + 1) * HT_],
                                        start=(q == 0 and r == 0 and g == 0), stop=True, skip_group_check=True)
                ins.then_inc(av_ok, 1)

            def transpose(b, q, n, banks):
                s = q % 2
                for j in banks:
                    if j == 0:
                        pe.wait_ge(k_in[s], (b * (NG // 2) + q // 2) * (16 * NP) + 16 * NP)
                    pe.wait_ge(kt_a if j % 2 == 0 else kt_v, n * 3 + j // 2 + 1)
                    for i in range(4):
                        x = 4 * j + i
                        ins = pe.transpose(KTP[(6 * q + j) % 4][:, i, :], KP[s][:, x // PAIRS, x % PAIRS * P:(x % PAIRS + 1) * P], ident[:, :])
                    ins.then_inc(kt_ps, 1)

            def group(b, q, n, nxt):
                s = q % 2
                first = isinstance(n, int) and n == 0
                pe.wait_ge(kt_a, n * 3 + 3 + 2)
                pe.wait_ge(kt_v, n * 3 + 3 + 2)
                pe.wait_ge(zb_ok, n + 1)
                for r in range(NP):
                    for g in range(PAIRS):
                        ins = pe.matmul(ZP[:, r, g * HT_:(g + 1) * HT_], KT[s][:, r * PAIRS + g, :],
                                        QD[:, bass.ds(b, 1), g, :].rearrange("p a c -> p (a c)"), start=True, stop=True)
                ins.then_inc(z_ok, 1)
                if not first:
                    cumulate(n - 1, 1 - s)
                if nxt:
                    transpose(*nxt, n + 1, (0, 1, 2, 3))
                if not first:
                    values(n - 1, (q - 1) % NG, b - 1 if q == 0 else b)
                if nxt:
                    transpose(*nxt, n + 1, (4, 5))

            transpose(0, 0, 0, range(6))
            sequences(group)(pe)
            cumulate(DB * NG - 1, 1)
            values(DB * NG - 1, NG - 1, DB - 1)


def mix_out_phase(nc, A, S, O):
    with ExitStack() as ctx:
        m = Mem(nc, ctx, "p3")
        W = m.sb("W", [P, KD, D])
        g_post = m.sb("g_post", [P, D])
        g_mlp = m.sb("g_mlp", [P, KD])
        eps = m.sb("eps", [P, 1])
        ident = m.sb("ident", [P, P])
        Y = [m.sb(f"Y{i}", [P, KD, P]) for i in range(2)]
        X = [m.sb(f"X{i}", [P, D]) for i in range(2)]
        V = m.sb("V", [P, D])
        X1 = [m.sb(f"X1{i}", [P, D]) for i in range(2)]
        XN = [m.sb(f"XN{i}", [P, D]) for i in range(2)]
        H = [m.sb(f"H{i}", [P, KD, P]) for i in range(2)]
        sq = m.sb("sq", [P, D])
        st = [m.sb(f"st{i}", [P, 6]) for i in range(2)]
        Z = [m.ps(f"Z{i}", [P, 2, 512]) for i in range(2)]
        HP = m.ps("HP", [P, 2, 512])
        w_in = m.sem("w_in")
        consts = m.sem("consts")
        passed = m.sem("passed")
        y_in = [m.sem(f"y_in{i}") for i in range(2)]
        z_ok = m.sem("z_ok")
        sq_ok = m.sem("sq_ok")
        root_ok = m.sem("root_ok")
        rec_ok = m.sem("rec_ok")
        v_ok = m.sem("v_ok")
        x1_ok = m.sem("x1_ok")
        xn_ok = m.sem("xn_ok")
        turned = m.sem("turned")
        h_ok = m.sem("h_ok")
        x1_out = [m.sem(f"x1_out{i}") for i in range(2)]
        h_out = [m.sem(f"h_out{i}") for i in range(2)]
        block = ctx.enter_context(nc.Block())

        def steps(eng, step):
            with eng.Fori(0, NT // 2) as i:
                for s in range(2):
                    step(i * 2 + s, s, i)
            step(NT, 0, NT // 2)

        @block.sync
        def _(sp):
            sp.dma_start(g_post[:, :], row_bcast(A["g_post_mix"], P)).then_inc(consts, 16)
            sp.dma_start(g_mlp[:, :], A["g_pre_mlp"].rearrange("(k p) -> p k", p=P),
                         allow_slow_non_contiguous=True).then_inc(consts, 16)
            sp.dma_start(W[:, :, :], A["w_out"].rearrange("(k p) n -> p k n", p=P)).then_inc(w_in, 16)

            def load(t, s):
                cols = bass.ds(t * P, P)
                sp.dma_start(Y[s][:, :, :], S["yT"][:, :, cols].rearrange("g p t -> p g t")).then_inc(y_in[s], 16)
                if isinstance(t, int) and t == NT:
                    for half in range(2):
                        sp.dma_start(X[s][half * NS:half * NS + NS, :], A["x_sample"][:, :]).then_inc(y_in[s], 16)
                else:
                    sp.dma_start(X[s][:, :], A["x_prompt"][cols, :]).then_inc(y_in[s], 16)

            load(0, 0)
            load(1, 1)

            def step(t, s, i, more=True):
                if more:
                    nxt = sp.snap((t + 2) * P) if not isinstance(t, int) else (t + 2) * P
                    sp.wait_ge(z_ok, t + 1)
                    wait_apart(sp, x1_ok, t + 1, passed)
                    load(t + 2, s)
                wait_apart(sp, x1_ok, t + 1, passed)
                sp.dma_start(S["x1"][bass.ds(t * P, P), :], X1[s][:, :]).then_inc(x1_out[s], 16)
                wait_apart(sp, h_ok, t + 2, passed)
                sp.dma_start(S["hT"][:, :, bass.ds(t * P, P)].rearrange("g p t -> p g t"), H[s][:, :, :]).then_inc(h_out[s], 16)

            with sp.Fori(0, NT // 2 - 1) as i:
                for s in range(2):
                    step(i * 2 + s, s, i)
            step(NT - 2, 0, NT // 2 - 1)
            step(NT - 1, 1, NT // 2 - 1, False)
            step(NT, 0, NT // 2, False)
            for s in range(2):
                sp.wait_ge(x1_out[s], 16 * (NT // 2 + 1 + (s == 0)))
                sp.wait_ge(h_out[s], 16 * (NT // 2 + 1 + (s == 0)))

        @block.gpsimd
        def _(pool):
            for s in range(2):
                pool.sem_inc(x1_out[s], 16)
                pool.sem_inc(h_out[s], 16)
            pool.memset(eps[:, :], EPS).then_inc(consts, 1)
            pool.memset(ident[:, :], 0.0).then_inc(consts, 1)
            pool.wait_ge(consts, 34)
            pool.affine_select(out=ident[:, :], in_=ident[:, :], compare_op=ALU.not_equal, fill=1.0, base=0,
                               pattern=[[-1, P]], channel_multiplier=1).then_inc(consts, 1)

        @block.scalar
        def _(act):
            act.wait_ge(consts, 35)

            def step(t, s, i):
                act.wait_ge(z_ok, t + 1)
                act.activation(sq[:, :], Z[s][:, :, :].rearrange("p a b -> p (a b)"), ACT.Square, accum_out=st[s][:, 0:1]).then_inc(sq_ok, 1)
                act.wait_ge(sq_ok, 2 * t + 1)
                act.activation(st[s][:, 1:2], st[s][:, 0:1], ACT.Sqrt, scale=1.0 / D, bias=eps[:, :]).then_inc(root_ok, 1)
                act.wait_ge(x1_ok, t + 1)
                act.activation(sq[:, :], X1[s][:, :], ACT.Square, accum_out=st[s][:, 3:4]).then_inc(sq_ok, 1)
                act.wait_ge(sq_ok, 2 * t + 2)
                act.activation(st[s][:, 4:5], st[s][:, 3:4], ACT.Sqrt, scale=1.0 / D, bias=eps[:, :]).then_inc(root_ok, 1)

            steps(act, step)

        @block.vector
        def _(dve):
            dve.sem_inc(h_ok, 1)
            dve.wait_ge(consts, 35)

            def step(t, s, i):
                dve.wait_ge(root_ok, 2 * t + 1)
                dve.reciprocal(st[s][:, 2:3], st[s][:, 1:2]).then_inc(rec_ok, 1)
                dve.wait_ge(rec_ok, 2 * t + 1)
                dve.scalar_tensor_tensor(out=V[:, :], in0=Z[s][:, :, :].rearrange("p a b -> p (a b)"), scalar=st[s][:, 2:3],
                                         in1=g_post[:, :], op0=ALU.mult, op1=ALU.mult).then_inc(v_ok, 1)
                dve.wait_ge(v_ok, t + 3)
                if isinstance(t, int) and t == NT:
                    dve.wait_ge(y_in[s], 32 * i + 48)
                else:
                    dve.wait_ge(y_in[s], 32 * i + 32)
                dve.wait_ge(x1_out[s], 16 * i + 16)
                dve.tensor_tensor(X1[s][:, :], V[:, :], X[s][:, :], ALU.add).then_inc(x1_ok, 1)
                dve.wait_ge(root_ok, 2 * t + 2)
                dve.reciprocal(st[s][:, 5:6], st[s][:, 4:5]).then_inc(rec_ok, 1)
                dve.wait_ge(rec_ok, 2 * t + 2)
                dve.tensor_scalar(XN[s][:, :], X1[s][:, :], st[s][:, 5:6], None, ALU.mult).then_inc(xn_ok, 1)
                dve.wait_ge(turned, t + 1)
                dve.wait_ge(h_out[s], 16 * i + 16)
                for h in range(2):
                    ins = dve.tensor_tensor(H[s][:, 4 * h:4 * h + 4, :], HP[:, h, :].rearrange("p (k t) -> p k t", k=4),
                                            g_mlp[:, 4 * h:4 * h + 4, None].broadcast_to([P, 4, P]), ALU.mult)
                ins.then_inc(h_ok, 1)

            steps(dve, step)

        @block.tensor
        def _(pe):
            pe.sem_inc(v_ok, 2)
            pe.wait_ge(consts, 35)
            pe.wait_ge(w_in, 16)

            def project(t, s, i):
                pe.wait_ge(y_in[s], 32 * i + 32 + (16 if isinstance(t, int) and t == NT else 0))
                pe.wait_ge(v_ok, t + 1)
                for h in range(2):
                    for k in range(KD):
                        ins = pe.matmul(Z[s][:, h, :], Y[s][:, k, :], W[:, k, h * 512:h * 512 + 512], start=(k == 0), stop=(k == KD - 1))
                ins.then_inc(z_ok, 1)

            def turn(t, s):
                pe.wait_ge(xn_ok, t + 1)
                pe.wait_ge(h_ok, t + 1)
                for k in range(KD):
                    ins = pe.transpose(HP[:, k // 4, (k % 4) * P:(k % 4 + 1) * P], XN[s][:, k * P:(k + 1) * P], ident[:, :])
                ins.then_inc(turned, 1)

            project(0, 0, 0)
            with pe.Fori(0, NT // 2 - 1) as i:
                for s in range(2):
                    project(i * 2 + s + 1, 1 - s, i + s)
                    turn(i * 2 + s, s)
            project(NT - 1, 1, NT // 2 - 1)
            turn(NT - 2, 0)
            project(NT, 0, NT // 2)
            turn(NT - 1, 1)
            turn(NT, 0)


def mlp_phase(nc, A, S, O):
    CH, NCH = 512, SEQ // 512
    assert 2 * NCH == DB
    RU, RD = 2, 4
    with ExitStack() as ctx:
        m = Mem(nc, ctx, "p4")
        g_post = m.sb("g_post", [P, D])
        eps = m.sb("eps", [P, 1])
        WU = [m.sb(f"WU{i}", [P, KD, P]) for i in range(RU)]
        WUH = [m.sb(f"WUH{i}", [P, KD, P], F32R) for i in range(RU)]
        WUL = [m.sb(f"WUL{i}", [P, KD, P], F32R) for i in range(RU)]
        WD = [m.sb(f"WD{i}", [P, CH]) for i in range(RD)]
        H = m.sb("H", [P, KD, CH])
        HI = m.sb("HI", [P, KD, CH], F32R)
        LO = m.sb("LO", [P, KD, CH], F32R)
        U = m.sb("U", [P, KF, CH])
        Z = [m.sb(f"Z{i}", [P, D]) for i in range(4)]
        X = [m.sb(f"X{i}", [P, D]) for i in range(4)]
        sq = m.sb("sq", [P, 512])
        st = [m.sb(f"st{i}", [P, 5]) for i in range(4)]
        UP = [m.ps(f"UP{i}", [P, CH]) for i in range(4)]
        ZP = [m.ps(f"ZP{i}", [P, 512]) for i in range(4)]
        consts = m.sem("consts")
        passed = m.sem("passed")
        moved = m.sem("moved")
        wu_in = [m.sem(f"wu_in{i}") for i in range(RU)]
        wd_in = [m.sem(f"wd_in{i}") for i in range(RD)]
        h_in = m.sem("h_in")
        x_in = m.sem("x_in")
        g_in = m.sem("g_in")
        hh_ok = m.sem("hh_ok")
        hl_ok = m.sem("hl_ok")
        wh_ok = m.sem("wh_ok")
        wl_ok = m.sem("wl_ok")
        dh_ok = m.sem("dh_ok")
        dl_ok = m.sem("dl_ok")
        r_ok = m.sem("r_ok")
        up_ok = m.sem("up_ok")
        u_ok = m.sem("u_ok")
        dn_step = m.sem("dn_step")
        zsq_ok = m.sem("zsq_ok")
        zc_ok = m.sem("zc_ok")
        sum_ok = m.sem("sum_ok")
        root_ok = m.sem("root_ok")
        rec_ok = m.sem("rec_ok")
        zn_ok = m.sem("zn_ok")
        y_ok = m.sem("y_ok")
        y_out = m.sem("y_out")
        y_free = m.sem("y_free")
        block = ctx.enter_context(nc.Block())

        @block.sync
        def _(sp):
            def up(c, f, slot, used):
                sp.wait_ge(used, c * KF + f + 1)
                sp.dma_start(WU[slot][:, :, :], A["w_up"][:, bass.ds(f * P, P)].rearrange("(k p) n -> p k n", p=P)).then_inc(wu_in[slot], 16)

            def down(c, h, f, slot):
                sp.wait_ge(dl_ok, (c * 2 + h) * KF + f + 1)
                sp.dma_start(WD[slot][:, :], A["w_down"][bass.ds(f * P, P), bass.ds(h * 512, 512)]).then_inc(wd_in[slot], 16)

            def chunk(c, used):
                with sp.Fori(0, KF // RU) as j:
                    for q in range(RU):
                        up(c, j * RU + q, q, used)
                for h in range(2):
                    with sp.Fori(0, KF // RD) as j:
                        for q in range(RD):
                            down(c, h, j * RD + q, q)

            with sp.Fori(0, NCH) as c:
                chunk(c, wl_ok)
            chunk(NCH, up_ok)

        @block.gpsimd
        def _(pool):
            pool.memset(eps[:, :], EPS).then_inc(consts, 1)
            for q in range(RU):
                pool.sem_inc(up_ok, 1)
            pool.sem_inc(dn_step, RD)

            with pool.Fori(0, NCH) as c:
                with pool.Fori(0, KF // RU) as j:
                    for q in range(RU):
                        wait_apart(pool, wu_in[q], (c * (KF // RU) + j) * 16 + 16, passed)
                        wait_apart(pool, up_ok, c * KF + j * RU + q + 1, passed)
                        pool.tensor_copy(WUH[q][:, :, :], WU[q][:, :, :]).then_inc(wh_ok, 1)

        @block.scalar
        def _(act):
            act.sem_inc(y_free, 1)
            act.sem_inc(r_ok, 4)
            act.sem_inc(zsq_ok, 4)
            act.dma_start(g_post[:, :], row_bcast(A["g_post_mlp"], P)).then_inc(g_in, 16)
            act.wait_ge(consts, 1)

            def load_h(c, n):
                act.wait_ge(hl_ok, c * (KD // 2))
                act.dma_start(H[:, :, 0:n], S["hT"][:, :, bass.ds(c * CH, n)].rearrange("g p t -> p g t")).then_inc(h_in, 16)

            def move(b, j):
                rows = (WIN - DT) // (KF // RD)
                for dst, src in (("s_wk", "cache_win_k"), ("s_wv", "cache_win_v")):
                    to = O[dst][bass.ds(b, 1), bass.ds(j * rows, rows), :].rearrange("b (a w) c -> (b a) (w c)", w=5)
                    of = A[src][bass.ds(b, 1), bass.ds(j * rows + DT, rows), :].rearrange("b (a w) c -> (b a) (w c)", w=5)
                    act.dma_start(to, of).then_inc(moved, 16)

            def high_h(c, n):
                act.wait_ge(h_in, c * 16 + 16)
                for k in range(0, KD, 2):
                    act.activation(HI[:, k:k + 2, 0:n], H[:, k:k + 2, 0:n], ACT.Copy).then_inc(hh_ok, 1)

            def load_x(c, tiles):
                for q in range(tiles):
                    act.dma_start(X[q][:, :], S["x1"][bass.ds(c * CH + q * P, P), :]).then_inc(x_in, 16)

            def chunk(c, tiles, n, nxt, dst, rows):
                with act.Fori(0, KF // 4) as j:
                    for q in range(4):
                        f = j * 4 + q
                        u = U[:, bass.ds(f, 1), 0:n].rearrange("p a n -> p (a n)")
                        wait_apart(act, up_ok, c * KF + f + 1 + RU, passed)
                        act.activation(u, UP[q][:, 0:n], ACT.Relu).then_inc(r_ok, 1)
                        wait_apart(act, r_ok, c * KF + f + 1 + 4, passed)
                        act.activation(u, u, ACT.Square).then_inc(u_ok, 1)
                if nxt:
                    load_h(c + 1, nxt[1])
                wait_apart(act, up_ok, c * KF + KF + RU, passed)
                wait_apart(act, u_ok, c * KF + KF, passed)
                for h in range(2):
                    with act.Fori(0, KF // RD) as j:
                        if n == CH:
                            move(c * 2 + h, j)
                        for q in range(RD):
                            wait_apart(act, dn_step, (c * 2 + h) * KF + j * RD + q + 1, passed)
                            wait_apart(act, wd_in[q], ((c * 2 + h) * (KF // RD) + j) * 16 + 16, passed)
                            u = U[:, bass.ds(j * RD + q, 1), 0:n].rearrange("p a n -> p (a n)")
                            act.activation(HI[:, q, 0:n], u, ACT.Copy)
                            act.activation(HI[:, RD + q, :], WD[q][:, :], ACT.Copy).then_inc(dh_ok, 1)
                    for q in range(tiles):
                        act.wait_ge(dn_step, (c * 2 + h + 1) * KF + RD)
                        act.wait_ge(zsq_ok, c * 8 + h * tiles + q + 4)
                        act.activation(sq[:, :], ZP[q][:, :], ACT.Square, accum_out=st[q][:, h:h + 1]).then_inc(zsq_ok, 1)
                if nxt and nxt[1] == CH:
                    high_h(c + 1, nxt[1])
                for q in range(tiles):
                    act.wait_ge(sum_ok, c * 4 + q + 1)
                    act.activation(st[q][:, 3:4], st[q][:, 2:3], ACT.Sqrt, scale=1.0 / D, bias=eps[:, :]).then_inc(root_ok, 1)
                for q in range(tiles):
                    act.wait_ge(y_ok, c * 4 + q + 1)
                    act.dma_start(dst(c, q), Z[q][0:rows, :]).then_inc(y_out, 16)
                if nxt:
                    load_x(c + 1, nxt[0])
                act.wait_ge(y_out, c * 64 + 16 * tiles)
                act.sem_inc(y_free, 1)

            to_prompt = lambda c, q: O["y_prompt"][bass.ds(c * CH + q * P, P), :]
            act.dma_start(H[:, :, :], S["hT"][:, :, 0:CH].rearrange("g p t -> p g t")).then_inc(h_in, 16)
            load_x(0, 4)
            high_h(0, CH)
            with act.Fori(0, NCH - 1) as c:
                chunk(c, 4, CH, (4, CH), to_prompt, P)
            chunk(NCH - 1, 4, CH, (1, P), to_prompt, P)
            chunk(NCH, 1, P, None, lambda c, q: O["y_sample"][:, :], NS)
            act.wait_ge(moved, 16 * 2 * DB * (KF // RD))

        @block.vector
        def _(dve):
            dve.sem_inc(wl_ok, RU)
            dve.sem_inc(dl_ok, RD)
            dve.sem_inc(zc_ok, 4)
            dve.wait_ge(g_in, 16)

            def split_h(c, n):
                for k in range(0, KD, 2):
                    dve.wait_ge(hh_ok, c * (KD // 2) + k // 2 + 1)
                    dve.tensor_tensor(LO[:, k:k + 2, 0:n], H[:, k:k + 2, 0:n], HI[:, k:k + 2, 0:n].bitcast(F32), ALU.subtract).then_inc(hl_ok, 1)

            def split_up(c, f, q):
                dve.wait_ge(wh_ok, c * KF + f + 1)
                dve.tensor_tensor(WUL[q][:, :, :], WU[q][:, :, :], WUH[q][:, :, :].bitcast(F32), ALU.subtract).then_inc(wl_ok, 1)

            def start(c, n):
                split_h(c, n)
                for q in range(RU):
                    split_up(c, q, q)

            def chunk(c, n, tiles, nxt):
                if n == CH:
                    with dve.Fori(1, KF // RU) as j:
                        for q in range(RU):
                            split_up(c, j * RU + q, q)
                wait_apart(dve, y_free, c + 1, passed)
                for h in range(2):
                    with dve.Fori(0, KF // RD) as j:
                        for q in range(RD):
                            wait_apart(dve, dh_ok, (c * 2 + h) * KF + j * RD + q + 1, passed)
                            u = U[:, bass.ds(j * RD + q, 1), 0:n].rearrange("p a n -> p (a n)")
                            dve.tensor_tensor(LO[:, q, 0:n], u, HI[:, q, 0:n].bitcast(F32), ALU.subtract)
                            dve.tensor_tensor(LO[:, RD + q, :], WD[q][:, :], HI[:, RD + q, :].bitcast(F32), ALU.subtract).then_inc(dl_ok, 1)
                    for q in range(tiles):
                        dve.wait_ge(zsq_ok, c * 8 + h * tiles + q + 1 + 4)
                        dve.tensor_copy(Z[q][:, h * 512:h * 512 + 512], ZP[q][:, :]).then_inc(zc_ok, 1)
                if nxt:
                    start(c + 1, CH)
                dve.wait_ge(x_in, c * 64 + 16 * tiles)
                dve.wait_ge(zc_ok, c * 8 + 2 * tiles + 4)
                for q in range(tiles):
                    dve.tensor_tensor(st[q][:, 2:3], st[q][:, 0:1], st[q][:, 1:2], ALU.add).then_inc(sum_ok, 1)
                for q in range(tiles):
                    n4 = c * 4 + q + 1
                    dve.wait_ge(root_ok, n4)
                    dve.reciprocal(st[q][:, 4:5], st[q][:, 3:4]).then_inc(rec_ok, 1)
                    dve.wait_ge(rec_ok, n4)
                    dve.scalar_tensor_tensor(out=Z[q][:, :], in0=Z[q][:, :], scalar=st[q][:, 4:5],
                                             in1=g_post[:, :], op0=ALU.mult, op1=ALU.mult).then_inc(zn_ok, 1)
                    dve.wait_ge(zn_ok, n4)
                    dve.tensor_tensor(Z[q][:, :], Z[q][:, :], X[q][:, :], ALU.add).then_inc(y_ok, 1)

            start(0, CH)
            with dve.Fori(0, NCH - 1) as c:
                chunk(c, CH, 4, CH)
            chunk(NCH - 1, CH, 4, None)
            chunk(NCH, P, 1, None)

        @block.tensor
        def _(pe):
            def product(out, hi, lo, rhi, rlo, first, last):
                pe.matmul(out, hi, rhi, start=first, stop=False)
                pe.matmul(out, hi, rlo, start=False, stop=False)
                return pe.matmul(out, lo, rhi, start=False, stop=last)

            def chunk(c, n, tiles):
                with pe.Fori(0, KF // 4) as j:
                    for q in range(4):
                        w = q % RU
                        pe.wait_ge(r_ok, c * KF + j * 4 + q + 1)
                        if n == CH:
                            pe.wait_ge(hl_ok, c * (KD // 2) + KD // 2)
                            pe.wait_ge(wl_ok, c * KF + j * 4 + q + 1 + RU)
                        else:
                            pe.wait_ge(h_in, c * 16 + 16)
                            pe.wait_ge(wu_in[w], (c * (KF // RU) + j * (4 // RU) + q // RU) * 16 + 16)
                        for k in range(KD):
                            if n == CH:
                                ins = product(UP[q][:, 0:n], WUH[w][:, k, :], WUL[w][:, k, :], HI[:, k, 0:n], LO[:, k, 0:n], k == 0, k == KD - 1)
                            else:
                                ins = pe.matmul(UP[q][:, 0:n], WU[w][:, k, :], H[:, k, 0:n], start=(k == 0), stop=(k == KD - 1))
                        ins.then_inc(up_ok, 1)
                for h in range(2):
                    pe.wait_ge(zc_ok, c * 8 + h * tiles + 4)
                    for f in range(KF):
                        pe.wait_ge(dl_ok, (c * 2 + h) * KF + f + 1 + RD)
                        s = f % RD
                        for q in range(tiles):
                            rows = slice(q * P, q * P + P)
                            ins = product(ZP[q][:, :], HI[:, s, rows], LO[:, s, rows], HI[:, RD + s, :], LO[:, RD + s, :], f == 0, f == KF - 1)
                        ins.then_inc(dn_step, 1)

            with pe.Fori(0, NCH) as c:
                chunk(c, CH, 4)
            chunk(NCH, P, 1)


def build(nc, A, O):
    S = {name: nc.dram_tensor(f"scratch_{name}", shape, F32).ap() for name, shape in (
        ("nat", (TP, NATC)),
        ("qkT", (GROUPS, P, TP)),
        ("br", (3, SEQ, NB + 2 * HB)),
        ("yT", (KD, P, TP)),
        ("x1", (TP, D)),
        ("hT", (KD, P, TP)))}
    project_phase(nc, A, S, O)
    stick_prompt_phase(nc, A, S, O)
    dilated_prompt_phase(nc, A, S, O)
    dilated_merge_phase(nc, A, S, O)
    mlstm_chunks(nc, A, S, O, False)
    mlstm_chunks(nc, A, S, O, True)
    dilated_sample_phase(nc, A, S, O)
    stick_sample_phase(nc, A, S, O)
    mix_out_phase(nc, A, S, O)
    mlp_phase(nc, A, S, O)


_INS = [("x_prompt", "x_prompt", (SEQ, D)), ("x_sample", "x_sample", (NS, D)),
        ("state_c", "state_mlstm_c", (DB, HA, HD, HD)), ("state_n", "state_mlstm_n", (DB, HA, HD)),
        ("state_m", "state_mlstm_m", (DB, HA)),
        ("cache_win_k", "cache_win_k", (DB, WIN, NB)), ("cache_win_v", "cache_win_v", (DB, WIN, NB)),
        ("cache_sb_k", "cache_sb_k", (-1, PAGE, NC)), ("cache_sb_v", "cache_sb_v", (-1, PAGE, NC)),
        ("page_table", "page_table", (DB, PAGES)),
        ("w_in", "w_in", (D, COLS)), ("b_igate", "b_igate", (HA,)), ("b_fgate", "b_fgate", (HA,)), ("b_sb", "b_sb", (HC,)),
        ("g_mlstm", "g_mlstm", (NA,)), ("w_out", "w_out", (D, D)),
        ("g_pre_mix", "g_pre_mix", (D,)), ("g_post_mix", "g_post_mix", (D,)),
        ("g_pre_mlp", "g_pre_mlp", (D,)), ("g_post_mlp", "g_post_mlp", (D,)),
        ("w_up", "w_up", (D, FF)), ("w_down", "w_down", (FF, D))]
_OUTS = [("y_prompt", (SEQ, D), (1, SEQ, D)), ("y_sample", (NS, D), (DB, DT, D)),
         ("p_c", (HA, HD, HD), (1, 1, HA, HD, HD)), ("p_n", (HA, HD), (1, 1, HA, HD)), ("p_m", (1, HA), (1, 1, HA)),
         ("p_wk", (SEQ, NB), (1, 1, SEQ, HB, HD)), ("p_wv", (SEQ, NB), (1, 1, SEQ, HB, HD)),
         ("p_sk", (SEQ, NC), (1, 1, SEQ, HC, HD)), ("p_sv", (SEQ, NC), (1, 1, SEQ, HC, HD)),
         ("s_c", (DB, HA, HD, HD), (1, DB, HA, HD, HD)), ("s_n", (DB, HA, HD), (1, DB, HA, HD)), ("s_m", (DB, HA), (1, DB, HA)),
         ("s_wk", (DB, WIN, NB), (1, DB, WIN, HB, HD)), ("s_wv", (DB, WIN, NB), (1, DB, WIN, HB, HD)),
         ("s_sk", (NS, NC), (1, DB, DT, HC, HD)), ("s_sv", (NS, NC), (1, DB, DT, HC, HD))]


def kernel(**inputs):
    import numpy as _np
    import concourse.bacc as _bacc
    from concourse.bass_utils import run_bass_kernel_spmd as _run

    nc = _bacc.Bacc("TRN2", target_bir_lowering=False, num_devices=1)
    arrays, A, O = {}, {}, {}
    for name, arg, shape in _INS:
        arrays[f"in_{name}"] = _np.ascontiguousarray(inputs[arg]).reshape(shape)
    cached, new = window_masks()
    arrays["in_window_mask"] = _np.concatenate([_np.array(cached, _np.float32), _np.array(new, _np.float32)], axis=1)
    for key, a in arrays.items():
        A[key[3:]] = nc.dram_tensor(key, a.shape, mybir.dt.from_np(a.dtype), kind="ExternalInput").ap()
    for name, shape, _ in _OUTS:
        O[name] = nc.dram_tensor(f"out_{name}", shape, F32, kind="ExternalOutput").ap()
    build(nc, A, O)
    r = _run(nc, [arrays], core_ids=[0])
    return tuple(_np.asarray(r.results[0][f"out_{name}"]).reshape(full) for name, _, full in _OUTS)
```
